# Optimizing a Trainium2 kernel written in Bass

```python
import jax, jax.numpy as jnp
from jax import lax
import numpy as np

D_MODEL = 1024
BATCH = 1
SEQ = 512
DEPTH = 2
DEC_BATCH = 1
DEC_SEQ = 32
PAST_LEN = 512

CHUNK = 64
BRANCH_W = 512
N_BRANCH = 3
CONV_CH = BRANCH_W
CONV_WIDTH = 31
SGU_CH = BRANCH_W
SGU_GROUPS = 4
SGU_GROUP_CH = SGU_CH // SGU_GROUPS
SGU_CHUNK = 128
SB_HEADS = 8
SB_HEAD_DIM = BRANCH_W // SB_HEADS
SB_WIDTH = SB_HEADS * SB_HEAD_DIM
SB_QBLOCK = 128
D_FF = 2816
FFN_CONV_WIDTH = 3
DN_ALPHA = (2 * DEPTH) ** 0.25
DN_BETA = (8 * DEPTH) ** -0.25
LN_EPS = 1e-5
OFF_A = 2 * CONV_CH
OFF_B = OFF_A + 2 * SGU_CH
OFF_C = OFF_B + 3 * SB_WIDTH
D_IN = OFF_C + N_BRANCH * D_MODEL
IN_SPLITS = (CONV_CH, OFF_A, OFF_A + SGU_CH, OFF_B, OFF_B + SB_WIDTH, OFF_B + 2 * SB_WIDTH, OFF_C)

kernel_name = 'hybrid_stream_encoder_step'

def layer_norm(x, g, b):
    xf = x.astype(jnp.float32)
    mu = jnp.mean(xf, axis=-1, keepdims=True)
    var = jnp.mean(jnp.square(xf - mu), axis=-1, keepdims=True)
    return ((xf - mu) * lax.rsqrt(var + LN_EPS) * g + b).astype(x.dtype)

def causal_dwconv(x_ext, w, b):
    ch = x_ext.shape[-1]
    y = lax.conv_general_dilated(x_ext, w[:, None, :].astype(x_ext.dtype), window_strides=(1,),
                                 padding='VALID', dimension_numbers=('NWC', 'WIO', 'NWC'),
                                 feature_group_count=ch)
    return y + b

def stick_breaking(q, k, v, q_pos, k_pos):
    z = jnp.einsum('bqhd,bkhd->bhqk', q, k, preferred_element_type=jnp.float32) * (SB_HEAD_DIM ** -0.5)
    mask = k_pos[None, :] < q_pos[:, None]
    log_keep = jnp.where(mask, jax.nn.log_sigmoid(-z), 0.0)
    later = lax.cumsum(log_keep, axis=3, reverse=True) - log_keep
    attn = jnp.where(mask, jnp.exp(jax.nn.log_sigmoid(z) + later), 0.0)
    return jnp.einsum('bhqk,bkhd->bqhd', attn.astype(v.dtype), v)

def stick_breaking_prompt(q, k, v):
    seq = q.shape[1]
    pos = jnp.arange(seq, dtype=jnp.int32)
    outs = []
    for i in range(seq // SB_QBLOCK):
        lo, hi = i * SB_QBLOCK, (i + 1) * SB_QBLOCK
        outs.append(stick_breaking(q[:, lo:hi], k[:, :hi], v[:, :hi], pos[lo:hi], pos[:hi]))
    return jnp.concatenate(outs, axis=1)

def spatial_gate(v, w_s, b_s):
    n_rows = v.shape[2]
    w = jnp.tril(w_s[:, :n_rows, :n_rows]).astype(v.dtype)
    return jnp.einsum('gts,bnsgc->bntgc', w, v) + b_s[:, :n_rows].T[None, None, :, :, None]

def trunk_layer(x, conv_hist, ffn_hist, k_hist, v_hist,
                w_in, b_gate, conv_w, conv_b, conv_ln_g, conv_ln_b,
                sgu_ln_g, sgu_ln_b, sgu_w, sgu_b, w_branch, w_out, ln1_g, ln1_b,
                w_up, ffn_conv_w, ffn_conv_b, w_down, ln2_g, ln2_b):
    bsz, t_len, _ = x.shape
    prompt = k_hist is None
    a_in, a_gate, u, v, q, k, vv, g = jnp.split(x @ w_in, IN_SPLITS, axis=-1)

    glu = a_in * jax.nn.sigmoid(a_gate)
    if prompt:
        conv_hist = jnp.zeros((bsz, CONV_WIDTH - 1, CONV_CH), glu.dtype)
    conv_ext = jnp.concatenate([conv_hist.astype(glu.dtype), glu], axis=1)
    y_a = jax.nn.silu(layer_norm(causal_dwconv(conv_ext, conv_w, conv_b), conv_ln_g, conv_ln_b))

    v_n = layer_norm(jax.nn.gelu(v, approximate=False), sgu_ln_g, sgu_ln_b)
    rows = SGU_CHUNK if prompt else t_len
    mixed = spatial_gate(v_n.reshape(bsz, t_len // rows, rows, SGU_GROUPS, SGU_GROUP_CH), sgu_w, sgu_b)
    y_b = jax.nn.gelu(u, approximate=False) * mixed.reshape(bsz, t_len, SGU_CH)

    q = q.reshape(bsz, t_len, SB_HEADS, SB_HEAD_DIM)
    k = k.reshape(bsz, t_len, SB_HEADS, SB_HEAD_DIM)
    vv = vv.reshape(bsz, t_len, SB_HEADS, SB_HEAD_DIM)
    if prompt:
        o = stick_breaking_prompt(q, k, vv)
    else:
        past = k_hist.shape[1]
        k_all = jnp.concatenate([k_hist.astype(k.dtype), k], axis=1)
        v_all = jnp.concatenate([v_hist.astype(vv.dtype), vv], axis=1)
        o = stick_breaking(q, k_all, v_all, past + jnp.arange(t_len, dtype=jnp.int32),
                           jnp.arange(past + t_len, dtype=jnp.int32))
    y_c = o.reshape(bsz, t_len, SB_WIDTH)

    gates = jax.nn.sigmoid(g.reshape(bsz, t_len, N_BRANCH, D_MODEL) + b_gate)
    merged = (gates[:, :, 0] * (y_a @ w_branch[0])
              + gates[:, :, 1] * (y_b @ w_branch[1])
              + gates[:, :, 2] * (y_c @ w_branch[2]))
    x = layer_norm(DN_ALPHA * x + merged @ w_out, ln1_g, ln1_b)

    f_gate, f_val = jnp.split(x @ w_up, 2, axis=-1)
    if prompt:
        ffn_hist = jnp.zeros((bsz, FFN_CONV_WIDTH - 1, D_FF), f_gate.dtype)
    ffn_ext = jnp.concatenate([ffn_hist.astype(f_gate.dtype), f_gate], axis=1)
    f = jax.nn.gelu(causal_dwconv(ffn_ext, ffn_conv_w, ffn_conv_b), approximate=False) * f_val
    x = layer_norm(DN_ALPHA * x + f @ w_down, ln2_g, ln2_b)
    return (x, conv_ext[:, -(CONV_WIDTH - 1):], ffn_ext[:, -(FFN_CONV_WIDTH - 1):], k, vv, v_n)

def setup_inputs(seed: int = 0) -> dict:
    key = jax.random.key(seed)
    keys = iter(jax.random.split(key, 32))

    def nrm(shape, scale):
        return scale * jax.random.normal(next(keys), shape, jnp.float32)

    return {
        'x_prompt': nrm((BATCH, SEQ, D_MODEL), 1.0),
        'x_sample': nrm((DEC_BATCH, DEC_SEQ, D_MODEL), 1.0),
        'cache_sb_k': nrm((DEPTH, DEC_BATCH, PAST_LEN, SB_HEADS, SB_HEAD_DIM), 1.0),
        'cache_sb_v': nrm((DEPTH, DEC_BATCH, PAST_LEN, SB_HEADS, SB_HEAD_DIM), 1.0),
        'state_conv_glu': nrm((DEPTH, DEC_BATCH, CONV_WIDTH - 1, CONV_CH), 0.5),
        'state_ffn_conv': nrm((DEPTH, DEC_BATCH, FFN_CONV_WIDTH - 1, D_FF), 1.0),
        'w_in': nrm((DEPTH, D_MODEL, D_IN), D_MODEL ** -0.5),
        'b_gate': nrm((DEPTH, N_BRANCH, D_MODEL), 0.01),
        'conv_w': nrm((DEPTH, CONV_WIDTH, CONV_CH), CONV_WIDTH ** -0.5),
        'conv_b': nrm((DEPTH, CONV_CH), 0.01),
        'conv_ln_g': 1.0 + nrm((DEPTH, CONV_CH), 0.01),
        'conv_ln_b': nrm((DEPTH, CONV_CH), 0.01),
        'sgu_ln_g': 1.0 + nrm((DEPTH, SGU_CH), 0.01),
        'sgu_ln_b': nrm((DEPTH, SGU_CH), 0.01),
        'sgu_w': nrm((DEPTH, SGU_GROUPS, SGU_CHUNK, SGU_CHUNK), SGU_CHUNK ** -0.5),
        'sgu_b': 1.0 + nrm((DEPTH, SGU_GROUPS, SGU_CHUNK), 0.01),
        'w_branch': nrm((DEPTH, N_BRANCH, BRANCH_W, D_MODEL), DN_BETA * BRANCH_W ** -0.5),
        'w_out': nrm((DEPTH, D_MODEL, D_MODEL), DN_BETA * D_MODEL ** -0.5),
        'ln1_g': 1.0 + nrm((DEPTH, D_MODEL), 0.01),
        'ln1_b': nrm((DEPTH, D_MODEL), 0.01),
        'w_up': nrm((DEPTH, D_MODEL, 2 * D_FF), D_MODEL ** -0.5),
        'ffn_conv_w': nrm((DEPTH, FFN_CONV_WIDTH, D_FF), FFN_CONV_WIDTH ** -0.5),
        'ffn_conv_b': nrm((DEPTH, D_FF), 0.01),
        'w_down': nrm((DEPTH, D_FF, D_MODEL), DN_BETA * D_FF ** -0.5),
        'ln2_g': 1.0 + nrm((DEPTH, D_MODEL), 0.01),
        'ln2_b': nrm((DEPTH, D_MODEL), 0.01),
    }

def reference(x_prompt, x_sample, cache_sb_k, cache_sb_v, state_conv_glu, state_ffn_conv,
              w_in, b_gate, conv_w, conv_b, conv_ln_g, conv_ln_b,
              sgu_ln_g, sgu_ln_b, sgu_w, sgu_b, w_branch, w_out, ln1_g, ln1_b,
              w_up, ffn_conv_w, ffn_conv_b, w_down, ln2_g, ln2_b):
    stacked = (w_in, b_gate, conv_w, conv_b, conv_ln_g, conv_ln_b,
               sgu_ln_g, sgu_ln_b, sgu_w, sgu_b, w_branch, w_out, ln1_g, ln1_b,
               w_up, ffn_conv_w, ffn_conv_b, w_down, ln2_g, ln2_b)
    x_p, x_s = x_prompt, x_sample
    p_k, p_v, p_conv, p_ffn = [], [], [], []
    s_k, s_v, s_conv, s_ffn, s_sgu = [], [], [], [], []
    for layer in range(DEPTH):
        lw = [w[layer] for w in stacked]
        x_p, c_new, f_new, k_new, v_new, _ = trunk_layer(x_p, None, None, None, None, *lw)
        p_k.append(k_new); p_v.append(v_new); p_conv.append(c_new); p_ffn.append(f_new)
        x_s, c_new, f_new, k_new, v_new, sgu_new = trunk_layer(
            x_s, state_conv_glu[layer], state_ffn_conv[layer],
            cache_sb_k[layer], cache_sb_v[layer], *lw)
        s_k.append(k_new); s_v.append(v_new); s_conv.append(c_new); s_ffn.append(f_new)
        s_sgu.append(sgu_new)
    new_sb_k_prompt = jnp.stack(p_k)
    new_sb_v_prompt = jnp.stack(p_v)
    new_conv_glu_prompt = jnp.stack(p_conv)
    new_ffn_conv_prompt = jnp.stack(p_ffn)
    new_sb_k_sample = jnp.stack(s_k)
    new_sb_v_sample = jnp.stack(s_v)
    new_conv_glu_sample = jnp.stack(s_conv)
    new_ffn_conv_sample = jnp.stack(s_ffn)
    new_sgu_v_sample = jnp.stack(s_sgu)
    return (x_p, x_s, new_sb_k_prompt, new_sb_v_prompt, new_conv_glu_prompt, new_ffn_conv_prompt,
            new_sb_k_sample, new_sb_v_sample, new_conv_glu_sample, new_ffn_conv_sample, new_sgu_v_sample)


_drawn_inputs = setup_inputs


def setup_inputs(seed=0):
    import zlib

    import numpy as np

    out = dict(_drawn_inputs(seed))
    spreads = {}
    factors = {'cache_sb_k': 6.324,
     'cache_sb_v': 2.79,
     'b_gate': 8.0,
     'conv_b': 8.0,
     'conv_ln_g': 60.556,
     'conv_ln_b': 58.441,
     'sgu_ln_g': 185.21,
     'sgu_ln_b': 179.195,
     'sgu_b': 134.153,
     'ln1_g': 10.589,
     'ln1_b': 17.364,
     'ffn_conv_b': 24.973,
     'ln2_g': 12.689,
     'ln2_b': 12.234}
    for name, (base, spread) in spreads.items():
        noise = np.random.default_rng([zlib.crc32(name.encode()), seed]).standard_normal(out[name].shape)
        drawn = base * np.exp(spread * noise) if base else spread * noise
        out[name] = __import__('jax').numpy.asarray(drawn.astype(out[name].dtype))
    for name, factor in factors.items():
        out[name] = (out[name] * factor).astype(out[name].dtype)
    return out
```

```python
from contextlib import ExitStack, contextmanager

import concourse.bass as bass
from concourse import mybir

F32 = mybir.dt.float32
F32R = mybir.dt.float32r
ALU = mybir.AluOpType
ACT = mybir.ActivationFunctionType
AX_X = mybir.AxisListType.X

P = 128
D = 1024
SEQ = 512
DEC = 32
T = SEQ + DEC
HALF = T // 2
BP = SEQ - HALF
KT = D // P
DEPTH = 2
CH = 512
CT = CH // P
WID = 31
HIST = WID - 1
PAST = 512
DH = 64
FF = 2816
FT = FF // P
GT = HIST + SEQ + HIST + DEC
CV = GT - HIST
SCOL = SEQ + HIST
GEX = 2 + SEQ + 2 + DEC
ALPHA = (2 * DEPTH) ** 0.25
EPS = 1e-5
CHUNK = 2048
WIN_CHUNKS = 26
UP_CHUNKS = 22
T4 = CT * T * 4

PAR = {}
_at = 0
for _n, _w in (("b_gate", 24), ("conv_w", WID * CT), ("conv_b", CT), ("conv_g", CT), ("conv_bb", CT),
               ("ln1_g", KT), ("ln1_b", KT), ("ln2_g", KT), ("ln2_b", KT), ("fw", 3 * FT), ("fb", FT)):
    PAR[_n] = _at
    _at += _w
NPAR = _at

UV_TAPS, B_TAPS, C_FIRST, C_TAPS = (2, 2, 2, 1), 5, 2, 2
KGROUPS = (4, 2, 4, 4, 4, 4)
assert sum(KGROUPS) == FT
STARTS_AT_1 = ("lo_full", "acc_free", "acc_full", "part_used", "sig_full", "o_hi", "layer_done", "m_sum", "vec",
               "yc_full", "att_full", "mixed_used")
assert sum(UV_TAPS) + 3 * B_TAPS + C_FIRST + 3 * C_TAPS == WID - 1


class Count:

    def __init__(self, name, adds):
        self.name, self.adds = name, adds
        self.n, self.loops = {}, []

    @staticmethod
    def starts_at(sem):
        return int(sem.name.rstrip("0123456789") in STARTS_AT_1)

    def seen(self, sem, back=0):
        v = self.n.get(sem.name, 0) - back + self.starts_at(sem)
        for i, key in self.loops:
            step = self.adds.get((self.name, key, sem.name), 0)
            if step:
                v = i * step + v
        return v

    def up(self, sem, by=1):
        self.n[sem.name] = self.n.get(sem.name, 0) + by
        return by

    def take(self, sem, by=1):
        self.up(sem, by)
        return self.seen(sem)

    def skip(self, sem, by=1):
        self.up(sem, by)

    def prev(self, sem):
        v = self.seen(sem)
        self.up(sem)
        return v

    @contextmanager
    def loop(self, key, n, i):
        start = dict(self.n)
        self.loops.append((i, key))
        yield
        self.loops.pop()
        for s, v in list(self.n.items()):
            add = v - start.get(s, 0)
            self.adds[(self.name, key, s)] = add
            self.n[s] = start.get(s, 0) + n * add


def row(tile, idx, a, b):
    if isinstance(idx, int):
        return tile[:, idx, a:b]
    return tile[:, bass.ds(idx, 1), a:b].rearrange("p o n -> p (o n)")


def col(tile, idx):
    if isinstance(idx, int):
        return tile[:, idx:idx + 1]
    return tile[:, bass.ds(idx, 1)]


def trunk(nc, adds, x_in, win, wbr, wout, wup, wdn, par_in, bc_in, sguw_in, kc_in, vc_in, gh_in, fh_in,
          y_out, k_out, v_out, glu_out, ffn_out, sgu_out):
    with ExitStack() as ctx:
        sems = {}

        def sem(name):
            sems[name] = ctx.enter_context(nc.semaphore(name))
            return sems[name]

        top = [(nc.sbuf_base + 31) // 32 * 32]

        def sb(name, shape, dt=F32, at=None):
            size = 4
            for s in shape[1:]:
                size *= s
            off = at
            if at is None:
                off = top[0]
                top[0] += (size + 31) // 32 * 32
            return nc.alloc_sbuf_tensor_at(name, shape, dt, offset=off)

        xT = sb("xT", [P, KT, T])
        xh = sb("xh", [P, KT, T], F32R)
        xl = sb("xl", [P, KT, T], F32R)
        raw = [sb(f"raw{s}", [P, CHUNK]) for s in range(2)]
        wh = [sb(f"wh{s}", [P, CHUNK], F32R) for s in range(2)]
        wl = [sb(f"wl{s}", [P, CHUNK], F32R) for s in range(2)]
        ident = sb("ident", [P, P])
        mean_d = sb("mean_d", [P, P])
        mean_c = sb("mean_c", [P, P])
        past1 = sb("past1", [P, P])
        past0 = sb("past0", [P, P])
        spast1 = sb("spast1", [P, DEC])
        spast0 = sb("spast0", [P, DEC])
        zero = sb("zero", [P, 1])
        eps = sb("eps", [P, 1])
        par = sb("par", [P, NPAR])
        st0 = sb("st0", [P, HALF])
        st1 = sb("st1", [P, HALF])
        st2 = sb("st2", [P, HALF])
        fst = sb("fst", [P, FT, 4])
        fhist = sb("fhist", [P, FT, 2])
        tmp = sb("tmp", [P, 4, HALF])
        wsgu = sb("wsgu", [P, CT, P])
        bc = sb("bc", [P, 3, CH])
        bnst = sb("bnst", [P, 5, 6])
        mv = sb("mv", [P, 5, 2])
        rs = sb("rs", [P, 2, 5])
        otmp = sb("otmp", [P, P])
        gex = sb("gex", [P, 2, GEX])
        cbuf = sb("cbuf", [P, 2, GEX - 2])
        F = top[0]
        assert F + 11 * T4 <= nc.sbuf_usable_end, F + 11 * T4
        fhh = [sb(f"fhh{h}", [P, FT, HALF], F32R, at=F + h * 2 * FT * HALF * 4) for h in range(2)]
        fll = [sb(f"fll{h}", [P, FT, HALF], F32R, at=F + (2 * h + 1) * FT * HALF * 4) for h in range(2)]
        yb = [sb(n, [P, CT, T], F32R, at=F + i * T4) for i, n in enumerate(("ybh", "ybl"))]
        q = sb("q", [P, CT, T], at=F)
        k = sb("k", [P, CT, T], at=F + T4)
        mh = sb("mh", [P, KT, T], F32R, at=F)
        yc = [sb(n, [P, CT, T], F32R, at=F + (2 + i) * T4) for i, n in enumerate(("ych", "ycl"))]
        ml = sb("ml", [P, KT, T], F32R, at=F + 2 * T4)
        merged = sb("merged", [P, KT, T], at=F + 4 * T4)
        kc = sb("kc", [P, CT, PAST], at=F + 4 * T4)
        vc = sb("vc", [P, CT, CH], at=F + 4 * T4 + CT * PAST * 4)
        gu = sb("gu", [P, CT, T], at=F + 4 * T4)
        sq = sb("sq", [P, KT, HALF], at=F + 39168)
        vtok = sb("vtok", [P, 5, CH], at=F + 6 * T4)
        ntok = sb("ntok", [P, 5, CH], at=F + 6 * T4)
        ya = [sb(n, [P, CT, T], F32R, at=F + (6 + i) * T4) for i, n in enumerate(("yah", "yal"))]
        vfm = sb("vfm", [P, CT, T], at=F + 62464)
        gv = sb("gv", [P, CT, T], at=F + 62464)
        glu = sb("glu", [P, CT, GT], at=F + 71168)
        acc = sb("acc", [P, CT, CV], at=F + 80832)
        keep = [sb(f"keep{i}", [P, T + 4], at=F + 80832 + i * 6976) for i in range(2)]
        beta = [sb(f"beta{i}", [P, T], at=F + 80832 + i * 6976 + 2208) for i in range(2)]
        att = [sb(f"att{i}", [P, 5 * P], at=F + 80832 + i * 6976 + 2208 + 2176) for i in range(2)]
        sqc = sb("sqc", [P, CT, HALF], at=F + 90016)

        ps = [ctx.enter_context(nc.psum_tensor(f"acc{b}", [P, 512], F32)) for b in range(4)]
        bs = [ctx.enter_context(nc.psum_tensor(f"score{b}", [P, 512], F32)) for b in range(2)]
        bt = ctx.enter_context(nc.psum_tensor("turned", [P, 512], F32))
        bo = ctx.enter_context(nc.psum_tensor("small", [P, 512], F32))

        x_loaded = sem("x_loaded")
        x_hi = sem("x_hi")
        consts = sem("consts")
        passed = sem("passed")
        raw_full = [sem(f"raw_full{s}") for s in range(2)]
        hi_full = [sem(f"hi_full{s}") for s in range(2)]
        lo_full = [sem(f"lo_full{s}") for s in range(2)]
        part_used = [sem(f"part_used{s}") for s in range(2)]
        acc_full = [sem(f"acc_full{b}") for b in range(4)]
        acc_free = [sem(f"acc_free{b}") for b in range(4)]
        x_ready = [sem(f"x_ready{h}") for h in range(2)]
        small_full = sem("small_full")
        layer_done = sem("layer_done")
        sgu_masked = sem("sgu_masked")
        kv_stored = sem("kv_stored")
        v_turned = sem("v_turned")
        vtok_full = sem("vtok_full")
        s_full = [sem(f"s_full{i}") for i in range(2)]
        sig_full = [sem(f"sig_full{i}") for i in range(2)]
        at_full = [sem(f"at_full{i}") for i in range(2)]
        t_full = sem("t_full")
        att_full = [sem(f"att_full{i}") for i in range(2)]
        o_full = sem("o_full")
        o_hi = sem("o_hi")
        yc_full = sem("yc_full")
        vec = sem("vec")
        glu_full = sem("glu_full")
        glu_stored = sem("glu_stored")
        gelu_v = sem("gelu_v")
        gelu_u = sem("gelu_u")
        tok_turned = sem("tok_turned")
        tok_full = sem("tok_full")
        tok_var = sem("tok_var")
        tok_std = sem("tok_std")
        ntok_full = sem("ntok_full")
        sgu_stored = sem("sgu_stored")
        mixed = sem("mixed")
        mixed_used = sem("mixed_used")
        yb_sum = sem("yb_sum")
        yb_hi = sem("yb_hi")
        yb_full = sem("yb_full")
        ln_sum = sem("ln_sum")
        ln_mean = sem("ln_mean")
        ln_cent = sem("ln_cent")
        ln_sq = sem("ln_sq")
        ln_ssum = sem("ln_ssum")
        ln_var = sem("ln_var")
        ln_std = sem("ln_std")
        ln_norm = sem("ln_norm")
        ln_hi = sem("ln_hi")
        ya_full = sem("ya_full")
        m_sum = sem("m_sum")
        m_hi = sem("m_hi")
        m_ready = [sem(f"m_ready{h}") for h in range(2)]
        gex_full = sem("gex_full")
        tap0_full = sem("tap0_full")
        conv3_full = sem("conv3_full")
        fgelu_full = sem("fgelu_full")
        f_hi = sem("f_hi")
        f_ready = sem("f_ready")
        ffn_stored = sem("ffn_stored")
        stored = sem("stored")

        QKV = (12, 13, 8, 9, 10, 11)
        GLU = (2, 0, 3, 1)
        UV = (6, 7, 4, 5)
        GATE = 14
        BRANCHES = (1, 2, 0)
        STEPS = 16

        def dcol(h):
            return slice(h * HALF, (h + 1) * HALF)

        block = ctx.enter_context(nc.Block())

        @block.sync
        def _(sp):
            c = Count("sp", adds)
            for s in sems.values():
                if c.starts_at(s):
                    sp.sem_inc(s, 1)
            sp.dma_start(xT[:, :, :], x_in).then_inc(x_loaded, 16)
            turn = [0]

            def chunk(src, size=CHUNK):
                s = turn[0] % 2
                turn[0] += 1
                sp.wait_ge(lo_full[s], c.prev(lo_full[s]))
                sp.dma_start(raw[s][:, 0:size], src).then_inc(raw_full[s], c.up(raw_full[s], 16))

            def flat(ap):
                return ap.rearrange("a p n -> (a p) n")

            with sp.Fori(0, DEPTH) as l, c.loop("layer", DEPTH, l):
                def w_in(i):
                    chunk(flat(win[bass.ds(l * WIN_CHUNKS + i, 1)]))

                for n in range(2):
                    w_in(QKV[n])
                sp.wait_ge(layer_done, c.prev(layer_done))
                for dst, src in ((par, par_in), (bc, bc_in), (wsgu, sguw_in), (kc, kc_in), (vc, vc_in),
                                 (fhist, fh_in)):
                    flat_dst = dst[:, :] if len(dst.shape) == 2 else dst[:, :, :].rearrange("p a n -> p (a n)")
                    sp.dma_start(flat_dst, flat(src[bass.ds(l, 1)])).then_inc(small_full, c.up(small_full, 16))
                for m in range(CT):
                    sp.dma_start(glu[:, m, SCOL:SCOL + HIST],
                                          flat(gh_in[bass.ds(l * CT + m, 1)])).then_inc(
                                              small_full, c.up(small_full, 16))
                for n in range(2, 6):
                    w_in(QKV[n])
                for n in range(4):
                    w_in(GLU[n])
                w_in(UV[0])
                for n in range(1, 3):
                    w_in(UV[n])
                sp.wait_ge(glu_full, c.take(glu_full, CT))
                for m in range(CT):
                    for j, a in enumerate((SEQ, GT - HIST)):
                        sp.dma_start(flat(glu_out[bass.ds(l * 2 * CT + 2 * m + j, 1)]), glu[:, m, a:a + HIST]).then_inc(
                            glu_stored, c.up(glu_stored, 16))
                w_in(UV[3])
                for n, b in enumerate(BRANCHES):
                    def pair(i, b=b):
                        w_in(GATE + 4 * b + i)
                        chunk(flat(wbr[bass.ds(l * 12 + 4 * b + i, 1)]), CHUNK // 2)
                    pair(0)
                    if n == 0:
                        sp.wait_ge(ntok_full, c.take(ntok_full))
                        sp.dma_start(flat(sgu_out[bass.ds(l, 1)]), ntok[0:DEC, 4, :]).then_inc(
                            sgu_stored, c.up(sgu_stored, 16))
                    with sp.Fori(0, 3) as i, c.loop(f"branch{n}", 3, i):
                        pair(i + 1)
                for h in range(2):
                    with sp.Fori(0, 2) as i, c.loop(f"out{h}", 2, i):
                        for j in range(2):
                            chunk(flat(wout[bass.ds(l * 4 + 2 * i + j, 1)]))
                with sp.Fori(0, 11) as i, c.loop("up", 11, i):
                    for j in range(2):
                        chunk(flat(wup[bass.ds(l * UP_CHUNKS + 11 * j + i, 1)]))
                for h in range(2):
                    if h == 1:
                        sp.wait_ge(conv3_full, c.take(conv3_full, FT))
                        sp.dma_start(flat(ffn_out[bass.ds(l, 1)]),
                                              fst[:, :, :].rearrange("p a n -> p (a n)")).then_inc(
                                                  ffn_stored, c.up(ffn_stored, 16))
                    with sp.Fori(0, 2) as i, c.loop(f"down{h}", 2, i):
                        at = 0
                        for kn in KGROUPS:
                            chunk(flat(wdn[bass.ds(l * 2 + i, 1), :, at * 512:(at + kn) * 512]), kn * 512)
                            at += kn
            chunk(win[0])
            for h in range(2):
                sp.wait_ge(x_ready[h], KT * (1 + 2 * DEPTH))
                sp.dma_start(y_out[:, :, dcol(h)], xT[:, :, dcol(h)]).then_inc(stored, 16)
            sp.wait_ge(stored, 32)
            sp.wait_ge(kv_stored, 32 * DEPTH)
            sp.wait_ge(glu_stored, 16 * 2 * CT * DEPTH)
            sp.wait_ge(sgu_stored, 16 * DEPTH)
            sp.wait_ge(ffn_stored, 16 * DEPTH)
            sp.wait_ge(raw_full[0], c.n[raw_full[0].name])

        @block.gpsimd
        def _(pool):
            c = Count("pool", adds)
            g = nc.gpsimd
            for t, v in ((ident, 0.0), (past1, 1.0), (past0, 1.0), (spast1, 1.0), (spast0, 1.0),
                         (mean_d, 1.0 / D), (mean_c, 1.0 / CH), (zero, 0.0), (eps, EPS), (mv, 1.0)):
                ap = t[:, :] if len(t.shape) == 2 else t[:, :, :]
                g.memset(ap, v).then_inc(consts, c.up(consts))
            g.memset(gex[:, :, :], 0.0).then_inc(consts, c.up(consts))
            pool.wait_ge(consts, c.seen(consts))

            def select(t, op, base, fill, rows=slice(0, P), n=P):
                g.affine_select(out=t[rows, 0:n], in_=t[rows, 0:n], compare_op=op, fill=fill, base=base,
                                         pattern=[[-1, n]], channel_multiplier=1).then_inc(consts, c.up(consts))
                pool.wait_ge(consts, c.seen(consts))

            select(ident, ALU.not_equal, 0, 1.0)
            select(past0, ALU.is_gt, 0, 0.0)
            for j in range(4):
                select(spast0, ALU.is_gt, 0, 0.0, slice(32 * j, 32 * j + 32), DEC)
            pool.wait_ge(consts, c.seen(consts))
            g.tensor_tensor(past1[:, :], past1[:, :], past0[:, :], ALU.subtract).then_inc(consts, c.up(consts))
            g.tensor_tensor(spast1[:, :], spast1[:, :], spast0[:, :], ALU.subtract).then_inc(consts, c.up(consts))
            turn = [0]

            def chunk(size=CHUNK):
                s = turn[0] % 2
                turn[0] += 1
                pool.wait_ge(hi_full[s], c.take(hi_full[s]))
                g.tensor_tensor(wl[s][:, 0:size], raw[s][:, 0:size], wh[s][:, 0:size].bitcast(F32),
                                         ALU.subtract).then_inc(lo_full[s], c.up(lo_full[s]))

            with pool.Fori(0, DEPTH) as r, c.loop("layer", DEPTH, r):
                for n in range(4):
                    chunk()
                pool.wait_ge(small_full, c.take(small_full, 160))
                pool.sem_inc(passed, 1)
                g.affine_select(out=wsgu[:, :, :], in_=wsgu[:, :, :], compare_op=ALU.is_ge, fill=0.0, base=0,
                                         pattern=[[0, CT], [1, P]], channel_multiplier=-1).then_inc(
                                             sgu_masked, c.up(sgu_masked))
                for n in range(10):
                    chunk()
                for n in range(3):
                    chunk()
                    chunk(CHUNK // 2)
                    with pool.Fori(0, 3) as r, c.loop(f"branch{n}", 3, r):
                        chunk()
                        chunk(CHUNK // 2)
                for h in range(2):
                    with pool.Fori(0, 2) as r, c.loop(f"out{h}", 2, r):
                        chunk()
                        chunk()
                with pool.Fori(0, 11) as r, c.loop("up", 11, r):
                    chunk()
                    chunk()
                for h in range(2):
                    with pool.Fori(0, 2) as r, c.loop(f"down{h}", 2, r):
                        for kn in KGROUPS:
                            chunk(kn * 512)

        @block.scalar
        def _(act):
            c = Count("act", adds)
            A = act.activation
            turn = [0]

            def hi(size=CHUNK, used=None):
                s = turn[0] % 2
                turn[0] += 1
                if used is not None:
                    act.wait_ge(used, c.seen(used))
                act.wait_ge(raw_full[s], c.take(raw_full[s], 16))
                A(wh[s][:, 0:size], raw[s][:, 0:size], ACT.Copy).then_inc(hi_full[s], c.up(hi_full[s]))

            def ln_squares(nt, src, buf):
                for j in range(2):
                    act.wait_ge(ln_cent, c.take(ln_cent))
                    n = nt // 2
                    A(buf[:, j * n:(j + 1) * n, :], src[:, j * n:(j + 1) * n], ACT.Square).then_inc(ln_sq, c.up(ln_sq))

            def ln_root():
                act.wait_ge(ln_var, c.take(ln_var))
                A(st1[:, :], bo[:, 0:HALF], ACT.Sqrt, bias=eps[:, 0:1]).then_inc(ln_std, c.up(ln_std))

            def ln_write(nt, buf, dst, gname, bname, fn, h):
                for t in range(nt):
                    if t % (nt // 2) == 0:
                        act.wait_ge(ln_norm, c.take(ln_norm))
                    A(dst[:, t, dcol(h)], buf[:, t, :], fn, scale=col(par, PAR[gname] + t),
                               bias=col(par, PAR[bname] + t)).then_inc(ln_hi, c.up(ln_hi))

            def sig(b, n):
                act.wait_ge(s_full[b], c.take(s_full[b]))
                A(keep[b][:, 0:n], bs[b][:, 0:n], ACT.Sigmoid, scale=-DH ** -0.5)
                A(beta[b][:, 0:n], bs[b][:, 0:n], ACT.Sigmoid, scale=DH ** -0.5).then_inc(
                    sig_full[b], c.up(sig_full[b]))

            def turned(b, n):
                act.wait_ge(t_full, c.take(t_full))
                A(att[b][:, 0:n], bt[:, 0:n], ACT.Copy).then_inc(att_full[b], c.up(att_full[b]))

            def out_rows(u):
                act.wait_ge(o_full, c.take(o_full))
                ht, i = u // 4, u % 4
                A(yc[0][:, ht, i * P:(i + 1) * P], bo[:, 0:P], ACT.Copy)
                if u > 0:
                    act.wait_ge(yc_full, c.seen(yc_full))
                c.skip(yc_full)
                A(otmp[:, :], bo[:, 0:P], ACT.Copy).then_inc(o_hi, c.up(o_hi))

            def step(n, end):
                if not end:
                    if 1 <= n <= STEPS:
                        turned(0, ((n - 1) % 4 + 1) * P)
                    if 2 <= n <= STEPS + 1:
                        out_rows(n - 2)
                    if n < STEPS:
                        sig(0, (n % 4 + 1) * P)
                else:
                    if 1 <= n <= STEPS:
                        turned(1, ((n - 1) % 4 + 1) * P)
                    if n < STEPS:
                        sig(1, (n % 4 + 1) * P)

            def sample_sig(s):
                for b, (lo_, n) in enumerate(((0, PAST), (PAST, DEC))):
                    act.wait_ge(s_full[b], c.take(s_full[b]))
                    A(keep[s][:, lo_:lo_ + n], bs[b][:, 0:n], ACT.Sigmoid, scale=-DH ** -0.5)
                    A(beta[s][:, lo_:lo_ + n], bs[b][:, 0:n], ACT.Sigmoid, scale=DH ** -0.5).then_inc(
                        sig_full[b], c.up(sig_full[b]))

            def sample_turned(s):
                act.wait_ge(t_full, c.take(t_full))
                A(att[s][:, 0:PAST], bt[:, 0:PAST], ACT.Copy).then_inc(att_full[s], c.up(att_full[s]))
                act.wait_ge(t_full, c.take(t_full))
                A(att[s][0:DEC, PAST:PAST + P], bt[0:DEC, 0:P], ACT.Copy).then_inc(att_full[s], c.up(att_full[s]))

            def plain(dst, m, b, sig_to, fn=ACT.Copy):
                h = b // 2
                act.wait_ge(acc_full[b], c.take(acc_full[b]))
                A(dst[:, m, dcol(h)], ps[b][:, 0:HALF], fn).then_inc(acc_free[b], c.up(acc_free[b]))

            act.wait_ge(x_loaded, 16)
            for h in range(2):
                for t in range(KT):
                    A(xh[:, t, dcol(h)], xT[:, t, dcol(h)], ACT.Copy).then_inc(x_hi, c.up(x_hi))
            hi()

            with act.Fori(0, DEPTH) as l, c.loop("layer", DEPTH, l):
                for n in range(6):
                    hi(used=acc_full[3])
                    for b in range(4):
                        dst = (vfm, q, k)[n // 2]
                        h, m = b // 2, 2 * (n % 2) + b % 2
                        act.wait_ge(acc_full[b], c.take(acc_full[b]))
                        A(dst[:, m, dcol(h)], ps[b][:, 0:HALF], ACT.Copy).then_inc(acc_free[b], c.up(acc_free[b]))
                for b in range(4):
                    act.wait_ge(acc_free[b], c.seen(acc_free[b]))
                for dst, src in ((k_out, k), (v_out, vfm)):
                    act.dma_start(dst[bass.ds(l, 1)].rearrange("a p n -> (a p) n"),
                                           src[:, :, :].rearrange("p a n -> p (a n)")).then_inc(
                                               kv_stored, c.up(kv_stored, 16))
                act.wait_ge(small_full, c.take(small_full, 160))
                for n in range(4):
                    hi(used=acc_full[3])
                    for b in range(4):
                        step(4 * n + b, False)
                        if n % 2 == 0:
                            act.wait_ge(acc_full[b], c.take(acc_full[b]))
                            A(tmp[:, b, :], ps[b][:, 0:HALF], ACT.Sigmoid).then_inc(acc_free[b], c.up(acc_free[b]))
                        else:
                            c.skip(acc_full[b])
                            c.skip(acc_free[b])
                        step(4 * n + b, True)
                act.wait_ge(kv_stored, c.seen(kv_stored))
                hi(used=acc_full[3])
                for b in range(4):
                    n = STEPS + b
                    step(n, False)
                    if b < 2:
                        sample_sig(b)
                    if 1 <= b < 3:
                        sample_turned(b - 1)
                    plain(gv, b % 2, b, None)
                    step(n, True)
                act.wait_ge(o_full, c.take(o_full))
                A(yc[0][:, :, SEQ:T], bo[:, 0:P].rearrange("p (a n) -> p a n", a=CT), ACT.Copy)
                act.wait_ge(yc_full, c.seen(yc_full))
                c.skip(yc_full)
                A(otmp[:, :], bo[:, 0:P], ACT.Copy).then_inc(o_hi, c.up(o_hi))
                act.wait_ge(acc_free[3], c.seen(acc_free[3]))
                A(gv[:, 0:2, :], gv[:, 0:2, :], ACT.Gelu).then_inc(gelu_v, c.up(gelu_v))
                for n in range(1, 4):
                    hi(used=acc_full[3])
                    for b in range(4):
                        plain(gv if n == 1 else gu, 2 * (n % 2) + b % 2, b, None, ACT.Gelu)
                act.wait_ge(tok_var, c.take(tok_var))
                A(rs[:, 0, :], mv[:, :, 1:2].rearrange("p a o -> p (a o)"), ACT.Sqrt, bias=eps[:, 0:1]).then_inc(
                    tok_std, c.up(tok_std))

                def gates(i, n, after=None):
                    hi(CHUNK // 2, used=acc_full[3])
                    act.wait_ge(m_sum, c.seen(m_sum))
                    for b in range(4):
                        act.wait_ge(acc_full[b], c.take(acc_full[b]))
                        act.sem_inc(passed, 1)
                        A(tmp[:, b, :], ps[b][:, 0:HALF], ACT.Sigmoid,
                                   bias=col(par, PAR["b_gate"] + 8 * BRANCHES[n] + 2 * i + b % 2)).then_inc(
                                       acc_free[b], c.up(acc_free[b]))
                        if after:
                            after(b)

                def products(i, n):
                    hi(used=acc_full[3])
                    for b in range(4):
                        c.skip(acc_full[b])
                        c.skip(acc_free[b])
                        if n == 1:
                            c.skip(m_sum)
                        if n == 2:
                            act.wait_ge(m_sum, c.take(m_sum))
                            A(row(mh, 2 * i + b % 2, *((b // 2) * HALF, (b // 2 + 1) * HALF)),
                                       row(merged, 2 * i + b % 2, *((b // 2) * HALF, (b // 2 + 1) * HALF)),
                                       ACT.Copy).then_inc(m_hi, c.up(m_hi))

                for n in range(3):
                    if n == 0:
                        gates(0, n)
                        for g_ in range(CT):
                            act.wait_ge(yb_sum, c.take(yb_sum))
                            A(yb[0][:, g_, :], gv[:, g_, :], ACT.Copy).then_inc(yb_hi, c.up(yb_hi))
                        products(0, n)
                    elif n == 2:
                        def conv_norm(b):
                            h = b // 2
                            if b % 2 == 0:
                                ln_squares(CT, acc_view(acc, h), sqc)
                                return
                            ln_root()
                            for t in range(CT):
                                if t % 2 == 0:
                                    act.wait_ge(ln_norm, c.take(ln_norm))
                                A(acc[:, t, dcol(h)], sqc[:, t, :], ACT.Silu, scale=col(par, PAR["conv_g"] + t),
                                  bias=col(par, PAR["conv_bb"] + t))
                                A(ya[0][:, t, dcol(h)], sqc[:, t, :], ACT.Silu,
                                           scale=col(par, PAR["conv_g"] + t), bias=col(par, PAR["conv_bb"] + t)).then_inc(
                                               ln_hi, c.up(ln_hi))

                        act.wait_ge(glu_stored, c.take(glu_stored, 16 * 2 * CT))
                        act.wait_ge(sgu_stored, c.take(sgu_stored, 16))
                        gates(0, n, conv_norm)
                        products(0, n)
                    else:
                        gates(0, n)
                        products(0, n)
                    with act.Fori(0, 3) as i, c.loop(f"branch{n}", 3, i):
                        gates(i + 1, n)
                        products(i + 1, n)

                def skip(bs_):
                    for b in bs_:
                        c.skip(acc_full[b])
                        c.skip(acc_free[b])

                with act.Fori(0, 2) as r, c.loop("out0", 2, r):
                    hi(used=acc_full[3])
                    skip((0, 1))
                    hi(used=acc_full[1])
                    skip((2, 3))
                hi(used=acc_full[3])
                skip((0, 1))
                ln_squares(KT, xT[:, :, dcol(0)], sq)
                hi(used=acc_full[1])
                skip((2, 3))
                hi(used=acc_full[3])
                ln_root()
                ln_write(KT, sq, xh, "ln1_g", "ln1_b", ACT.Identity, 0)
                skip((0, 1))
                hi(used=acc_full[1])
                skip((2, 3))

                def gate_rows(b):
                    m = b % 2
                    act.wait_ge(acc_full[b], c.take(acc_full[b]))
                    if b < 2:
                        A(gex[:, m, 2:2 + HALF], ps[b][:, 0:HALF], ACT.Copy).then_inc(acc_free[b], c.up(acc_free[b]))
                    else:
                        A(gex[:, m, 2 + HALF:2 + SEQ], ps[b][:, 0:BP], ACT.Copy)
                        A(gex[:, m, 4 + SEQ:GEX], ps[b][:, BP:HALF], ACT.Copy).then_inc(acc_free[b], c.up(acc_free[b]))

                def conv_open(i):
                    act.wait_ge(acc_free[3], c.seen(acc_free[3]))
                    act.wait_ge(gex_full, c.take(gex_full, 2))
                    for m in range(2):
                        t = 2 * i + m
                        A(cbuf[:, m, :], gex[:, m, 0:GEX - 2], ACT.Identity, scale=col(par, PAR["fw"] + t),
                                   bias=col(par, PAR["fb"] + t)).then_inc(tap0_full, c.up(tap0_full))
                    for m in range(2):
                        act.wait_ge(conv3_full, c.take(conv3_full))
                        A(cbuf[:, m, :], cbuf[:, m, :], ACT.Gelu).then_inc(fgelu_full, c.up(fgelu_full))

                def f_rows(i, b):
                    c.skip(acc_full[b])
                    act.wait_ge(acc_free[b], c.take(acc_free[b]))
                    A(row(fhh[b // 2], 2 * i + b % 2, 0, HALF), tmp[:, b, :], ACT.Copy).then_inc(f_hi, c.up(f_hi))

                hi(used=acc_full[3])
                gate_rows(0)
                gate_rows(1)
                ln_squares(KT, xT[:, :, dcol(1)], sq)
                ln_root()
                ln_write(KT, sq, xh, "ln1_g", "ln1_b", ACT.Identity, 1)
                gate_rows(2)
                gate_rows(3)
                hi(used=acc_full[3])
                conv_open(0)
                for b in range(4):
                    f_rows(0, b)
                with act.Fori(0, 10) as i, c.loop("up", 10, i):
                    hi(used=acc_full[3])
                    for b in range(4):
                        gate_rows(b)
                    hi(used=acc_full[3])
                    conv_open(i + 1)
                    for b in range(4):
                        f_rows(i + 1, b)

                def down(i, middle=()):
                    for j in range(len(KGROUPS)):
                        nxt = KGROUPS[(j + 1) % len(KGROUPS)] * 512
                        hi(nxt, used=acc_full[3] if j == 0 else part_used[(j - 1) % 2])
                        if j < len(KGROUPS) - 1:
                            c.skip(part_used[j % 2])
                        if j < len(middle):
                            middle[j]()
                    skip(range(4))

                with act.Fori(0, 2) as r, c.loop("down0", 2, r):
                    down(0)
                down(0, (lambda: ln_squares(KT, xT[:, :, dcol(0)], sq), ln_root,
                         lambda: ln_write(KT, sq, xh, "ln2_g", "ln2_b", ACT.Identity, 0)))
                down(1)
                ln_squares(KT, xT[:, :, dcol(1)], sq)
                ln_root()
                ln_write(KT, sq, xh, "ln2_g", "ln2_b", ACT.Identity, 1)

        @block.vector
        def _(dve):
            c = Count("dve", adds)
            v = nc.vector

            dve.wait_ge(consts, 19)
            for h in range(2):
                for t in range(KT):
                    dve.wait_ge(x_hi, c.take(x_hi))
                    v.tensor_tensor(xl[:, t, dcol(h)], xT[:, t, dcol(h)], xh[:, t, dcol(h)].bitcast(F32),
                                             ALU.subtract).then_inc(x_ready[h], c.up(x_ready[h]))

            def ln_open(nt, src):
                dve.wait_ge(vec, c.seen(vec))
                v.tensor_reduce(st0[:, :], src.rearrange("p k t -> p t k"), AX_X, ALU.add).then_inc(
                    ln_sum, c.up(ln_sum))

            def ln_centre(nt, src):
                dve.wait_ge(ln_mean, c.take(ln_mean))
                n = nt // 2
                for j in range(2):
                    mean = bo[:, 0:HALF].unsqueeze(1).broadcast_to([P, n, HALF])
                    part = src[:, j * n:(j + 1) * n]
                    v.tensor_tensor(part, part, mean, ALU.subtract).then_inc(ln_cent, c.up(ln_cent))

            def ln_squares(nt, buf):
                dve.wait_ge(ln_sq, c.take(ln_sq, 2))
                v.tensor_reduce(st0[:, :], buf[:, 0:nt, :].rearrange("p k t -> p t k"), AX_X, ALU.add).then_inc(
                    ln_ssum, c.up(ln_ssum))

            def ln_norm_(nt, src, buf):
                dve.wait_ge(ln_std, c.take(ln_std))
                v.reciprocal(st2[:, :], st1[:, :]).then_inc(vec, c.up(vec))
                dve.wait_ge(vec, c.seen(vec))
                n = nt // 2
                for j in range(2):
                    r = st2[:, :].unsqueeze(1).broadcast_to([P, n, HALF])
                    v.tensor_tensor(buf[:, j * n:(j + 1) * n, :], src[:, j * n:(j + 1) * n], r, ALU.mult).then_inc(
                        ln_norm, c.up(ln_norm))

            def ln_value(gname, bname, h):
                dve.wait_ge(ln_norm, c.seen(ln_norm))
                for t in range(KT):
                    v.tensor_scalar(xT[:, t, dcol(h)], sq[:, t, :], col(par, PAR[gname] + t),
                                        col(par, PAR[bname] + t), ALU.mult, ALU.add).then_inc(vec, c.up(vec))

            def ln_lo(h):
                dve.wait_ge(vec, c.seen(vec))
                for t in range(KT):
                    dve.wait_ge(ln_hi, c.take(ln_hi))
                    v.tensor_tensor(xl[:, t, dcol(h)], xT[:, t, dcol(h)], xh[:, t, dcol(h)].bitcast(F32),
                                             ALU.subtract).then_inc(x_ready[h], c.up(x_ready[h]))

            def skip(bs_):
                for b in bs_:
                    c.skip(acc_full[b])
                    c.skip(acc_free[b])

            def attend(b, n, m1, m0, w):
                dve.wait_ge(sig_full[b], c.take(sig_full[b]))
                weights(b, n, m1, m0, w, b)

            def weights(b, n, m1, m0, w, done):
                v.tensor_tensor(keep[b][:, n - w:n], keep[b][:, n - w:n], m1[:, 0:w], ALU.max).then_inc(vec, c.up(vec))
                v.tensor_tensor(beta[b][:, n - w:n], beta[b][:, n - w:n], m0[:, 0:w], ALU.mult).then_inc(vec, c.up(vec))
                v.memset(keep[b][:, n:n + 1], 1.0).then_inc(vec, c.up(vec))
                dve.wait_ge(vec, c.seen(vec))
                back = slice(n - 1, None, -1)
                v.tensor_tensor_scan(keep[b][:, 0:n][:, ::-1], keep[b][:, 0:n][:, ::-1],
                                         zero[:, 0:1].broadcast_to([P, n]), 1.0, ALU.mult, ALU.add).then_inc(
                                             vec, c.up(vec))
                dve.wait_ge(vec, c.seen(vec))
                v.tensor_tensor(beta[b][:, 0:n], beta[b][:, 0:n], keep[b][:, 1:n + 1], ALU.mult).then_inc(
                    at_full[done], c.up(at_full[done]))

            def rows_lo(u):
                dve.wait_ge(o_hi, c.take(o_hi))
                ht, i = u // 4, u % 4
                cols = slice(i * P, (i + 1) * P)
                v.tensor_tensor(yc[1][:, ht, cols], otmp[:, :], yc[0][:, ht, cols].bitcast(F32), ALU.subtract).then_inc(
                    yc_full, c.up(yc_full))

            def step(n, end):
                if not end:
                    if n < STEPS:
                        attend(0, (n % 4 + 1) * P, past1, past0, P)
                else:
                    if n < STEPS:
                        attend(1, (n % 4 + 1) * P, past1, past0, P)
                    if 2 <= n <= STEPS + 1:
                        rows_lo(n - 2)

            def tap(j):
                for m in range(CT):
                    dve.wait_ge(vec, c.seen(vec, CT - 1))
                    v.scalar_tensor_tensor(out=acc[:, m, :], in0=glu_at(m, j), scalar=col(par, PAR["conv_w"] + j * CT + m),
                                               in1=acc[:, m, :], op0=ALU.mult, op1=ALU.add).then_inc(vec, c.up(vec))

            def glu_at(m, j):
                if isinstance(j, int):
                    return glu[:, m, j:j + CV]
                return glu[:, m, bass.ds(j, CV)]

            with dve.Fori(0, DEPTH) as r, c.loop("layer", DEPTH, r):
                dve.wait_ge(vec, c.seen(vec))
                v.memset(glu[:, :, 0:HIST], 0.0).then_inc(vec, c.up(vec))
                for n in range(6):
                    skip(range(4))
                for t in range(5):
                    dve.wait_ge(v_turned, c.take(v_turned))
                    n = P if t < 4 else DEC
                    v.tensor_copy(vtok[0:n, t, :], bt[0:n, :]).then_inc(vtok_full, c.up(vtok_full))
                dve.wait_ge(small_full, c.take(small_full, 160))
                for n in range(4):
                    for b in range(4):
                        step(4 * n + b, False)
                        if n % 2 == 0:
                            skip((b,))
                        else:
                            m = n // 2 * 2 + b % 2
                            dve.wait_ge(acc_free[b], c.seen(acc_free[b]))
                            dve.wait_ge(acc_full[b], c.take(acc_full[b]))
                            o = HIST + (b // 2) * HALF
                            if b < 2:
                                v.tensor_tensor(glu[:, m, o:o + HALF], ps[b][:, 0:HALF], tmp[:, b, :],
                                                         ALU.mult).then_inc(acc_free[b], c.up(acc_free[b]))
                            else:
                                v.tensor_tensor(glu[:, m, o:o + BP], ps[b][:, 0:BP], tmp[:, b, 0:BP], ALU.mult).then_inc(
                                    vec, c.up(vec))
                                v.tensor_tensor(glu[:, m, GT - DEC:GT], ps[b][:, BP:HALF], tmp[:, b, BP:HALF],
                                                         ALU.mult).then_inc(acc_free[b], c.up(acc_free[b]))
                        step(4 * n + b, True)
                for b in range(4):
                    n = STEPS + b
                    step(n, False)
                    if b < 2:
                        dve.wait_ge(sig_full[0], c.take(sig_full[0]))
                        dve.wait_ge(sig_full[1], c.take(sig_full[1]))
                        weights(b, PAST + DEC, spast1, spast0, DEC, b)
                    skip((b,))
                    step(n, True)
                dve.wait_ge(o_hi, c.take(o_hi))
                v.tensor_tensor(yc[1][:, :, SEQ:T], otmp[:, :].rearrange("p (a n) -> p a n", a=CT),
                                         yc[0][:, :, SEQ:T].bitcast(F32), ALU.subtract).then_inc(yc_full, c.up(yc_full))
                dve.wait_ge(at_full[1], c.seen(at_full[1]))
                dve.wait_ge(acc_free[3], c.seen(acc_free[3]))
                dve.wait_ge(vec, c.seen(vec))
                for m in range(CT):
                    v.tensor_scalar(acc[:, m, :], glu_at(m, 0), col(par, PAR["conv_w"] + m),
                                             col(par, PAR["conv_b"] + m), ALU.mult, ALU.add).then_inc(
                                                 glu_full, c.up(glu_full))
                dve.wait_ge(glu_full, c.seen(glu_full))
                at = 1
                for n in range(4):
                    if n > 0:
                        skip(range(4))
                    for _ in range(UV_TAPS[n]):
                        tap(at)
                        at += 1
                    if n == 2:
                        for t in range(5):
                            dve.wait_ge(tok_turned, c.take(tok_turned))
                            r = P if t < 4 else DEC
                            v.tensor_copy(ntok[0:r, t, :], bt[0:r, :]).then_inc(tok_full, c.up(tok_full))
                            dve.wait_ge(tok_full, c.seen(tok_full))
                            v.bn_stats(bnst[0:r, t, :], ntok[0:r, t, :]).then_inc(vec, c.up(vec))
                            dve.wait_ge(vec, c.seen(vec))
                            dve.sem_inc(passed, 1)
                            v.bn_aggr(mv[0:r, t, :], bnst[0:r, t, :]).then_inc(vec, c.up(vec))
                dve.wait_ge(vec, c.seen(vec))
                v.memset(rs[:, 1, :], 0.0).then_inc(tok_var, c.up(tok_var))
                dve.wait_ge(tok_std, c.take(tok_std))
                v.reciprocal(rs[:, 1, :], rs[:, 0, :]).then_inc(vec, c.up(vec))
                dve.wait_ge(vec, c.seen(vec))
                for t in (4, 0, 1, 2, 3):
                    r = P if t < 4 else DEC
                    v.tensor_scalar(ntok[0:r, t, :], ntok[0:r, t, :], mv[0:r, t, 0:1], rs[0:r, 1, t:t + 1],
                                        ALU.subtract, ALU.mult).then_inc(vec, c.up(vec))
                dve.wait_ge(vec, c.seen(vec))
                for t in (4, 0, 1, 2, 3):
                    r = P if t < 4 else DEC
                    v.tensor_tensor(ntok[0:r, t, :], ntok[0:r, t, :], bc[0:r, 0, :], ALU.mult).then_inc(vec, c.up(vec))
                dve.wait_ge(vec, c.seen(vec))
                for t in (0, 1, 2, 3, 4):
                    r = P if t < 4 else DEC
                    ins = v.tensor_tensor(ntok[0:r, t, :], ntok[0:r, t, :], bc[0:r, 1, :], ALU.add)
                    if t < 4:
                        ins.then_inc(vec, c.up(vec))
                    else:
                        ins.then_inc(ntok_full, c.up(ntok_full))
                for g_ in range(CT):
                    dve.wait_ge(mixed, c.take(mixed, 2 if g_ == 0 else 1))
                    bias = bc[:, 2, g_ * P:(g_ + 1) * P]
                    v.tensor_tensor(gv[:, g_, 0:SEQ].rearrange("p (a n) -> p a n", a=4),
                                        bs[g_ % 2][:, :].rearrange("p (a n) -> p a n", a=4),
                                        bias.unsqueeze(1).broadcast_to([P, 4, P]), ALU.add).then_inc(vec, c.up(vec))
                    v.tensor_tensor(gv[:, g_, SEQ:T], bt[:, g_ * DEC:(g_ + 1) * DEC],
                                             bias[:, 0:DEC], ALU.add).then_inc(mixed_used, c.up(mixed_used))
                    dve.wait_ge(mixed_used, c.seen(mixed_used))
                    dve.wait_ge(vec, c.seen(vec))
                    v.tensor_tensor(gv[:, g_, :], gv[:, g_, :], gu[:, g_, :], ALU.mult).then_inc(yb_sum, c.up(yb_sum))
                    dve.wait_ge(yb_sum, c.seen(yb_sum))
                for g_ in range(CT):
                    dve.wait_ge(yb_hi, c.take(yb_hi))
                    v.tensor_tensor(yb[1][:, g_, :], gv[:, g_, :], yb[0][:, g_, :].bitcast(F32),
                                             ALU.subtract).then_inc(yb_full, c.up(yb_full))

                def products(i, n):
                    for b in range(4):
                        skip((b,))
                    for b in range(4):
                        h, t = b // 2, 2 * i + b % 2
                        dve.wait_ge(acc_free[b], c.seen(acc_free[b]))
                        dve.wait_ge(acc_full[b], c.take(acc_full[b]))
                        cols = (h * HALF, (h + 1) * HALF)
                        if n == 0:
                            v.tensor_tensor(row(merged, t, *cols), ps[b][:, 0:HALF], tmp[:, b, :], ALU.mult).then_inc(
                                acc_free[b], c.up(acc_free[b]))
                        else:
                            v.tensor_tensor(tmp[:, b, :], ps[b][:, 0:HALF], tmp[:, b, :], ALU.mult).then_inc(
                                acc_free[b], c.up(acc_free[b]))
                            dve.wait_ge(acc_free[b], c.seen(acc_free[b]))
                            done = v.tensor_tensor(row(merged, t, *cols), row(merged, t, *cols), tmp[:, b, :], ALU.add)
                            done.then_inc(m_sum, c.up(m_sum))
                    if n == 2:
                        for b in range(4):
                            h, t = b // 2, 2 * i + b % 2
                            cols = (h * HALF, (h + 1) * HALF)
                            dve.wait_ge(m_hi, c.take(m_hi))
                            v.tensor_tensor(row(ml, t, *cols), row(merged, t, *cols),
                                                     row(mh, t, *cols).bitcast(F32), ALU.subtract).then_inc(
                                                         m_ready[h], c.up(m_ready[h]))

                products(0, 0)
                with dve.Fori(0, 3) as i, c.loop("branch0", 3, i):
                    for j in range(B_TAPS):
                        tap(i * B_TAPS + (at + j))
                    products(i + 1, 0)
                at += 3 * B_TAPS
                for j in range(C_FIRST):
                    tap(at + j)
                at += C_FIRST
                products(0, 1)
                with dve.Fori(0, 3) as i, c.loop("branch1", 3, i):
                    for j in range(C_TAPS):
                        tap(i * C_TAPS + (at + j))
                    products(i + 1, 1)
                dve.wait_ge(vec, c.seen(vec))
                v.tensor_copy(st2[:, 0:P].rearrange("p (a n) -> p a n", a=CT), acc[:, :, SCOL:SCOL + DEC]).then_inc(
                    vec, c.up(vec))
                dve.wait_ge(vec, c.seen(vec))
                v.tensor_copy(acc[:, :, SEQ:T], st2[:, 0:P].rearrange("p (a n) -> p a n", a=CT)).then_inc(
                    vec, c.up(vec))
                for h in range(2):
                    ln_open(CT, acc_view(acc, h))
                    ln_centre(CT, acc_view(acc, h))
                    ln_squares(CT, sqc)
                    ln_norm_(CT, acc_view(acc, h), sqc)
                    for t in range(CT):
                        dve.wait_ge(ln_hi, c.take(ln_hi))
                        v.tensor_tensor(ya[1][:, t, dcol(h)], acc[:, t, dcol(h)],
                                                 ya[0][:, t, dcol(h)].bitcast(F32), ALU.subtract).then_inc(
                                                     ya_full, c.up(ya_full))
                products(0, 2)
                with dve.Fori(0, 3) as i, c.loop("branch2", 3, i):
                    products(i + 1, 2)

                def residual(t, b, h):
                    cols = (h * HALF, (h + 1) * HALF)
                    dve.wait_ge(acc_full[b], c.take(acc_full[b]))
                    v.scalar_tensor_tensor(out=row(xT, t, *cols), in0=row(xT, t, *cols), scalar=ALPHA,
                                                    in1=ps[b][:, 0:HALF], op0=ALU.mult, op1=ALU.add).then_inc(
                                                        acc_free[b], c.up(acc_free[b]))

                x0, x1 = xT[:, :, dcol(0)], xT[:, :, dcol(1)]
                with dve.Fori(0, 2) as i, c.loop("out0", 2, i):
                    for b in range(4):
                        residual(4 * i + b, b, 0)
                dve.wait_ge(acc_free[3], c.seen(acc_free[3]))
                ln_open(KT, x0)
                residual(0, 0, 1)
                ln_centre(KT, x0)
                residual(1, 1, 1)
                ln_squares(KT, sq)
                residual(2, 2, 1)
                residual(3, 3, 1)
                ln_norm_(KT, x0, sq)
                ln_value("ln1_g", "ln1_b", 0)
                residual(4, 0, 1)
                ln_lo(0)
                for b in range(1, 4):
                    residual(4 + b, b, 1)
                dve.wait_ge(acc_free[3], c.seen(acc_free[3]))
                ln_open(KT, x1)
                ln_centre(KT, x1)
                ln_squares(KT, sq)
                ln_norm_(KT, x1, sq)
                ln_value("ln1_g", "ln1_b", 1)
                ln_lo(1)

                def conv_close(i):
                    skip(range(4))
                    for m in range(2):
                        t = 2 * i + m
                        dve.wait_ge(tap0_full, c.take(tap0_full))
                        v.scalar_tensor_tensor(out=cbuf[:, m, :], in0=gex[:, m, 1:GEX - 1],
                                                   scalar=col(par, PAR["fw"] + FT + t), in1=cbuf[:, m, :],
                                                   op0=ALU.mult, op1=ALU.add).then_inc(vec, c.up(vec))
                        v.tensor_copy(row(fst, t, 0, 2), gex[:, m, SEQ:SEQ + 2]).then_inc(vec, c.up(vec))
                        v.tensor_copy(row(fst, t, 2, 4), gex[:, m, GEX - 2:GEX]).then_inc(vec, c.up(vec))
                        dve.wait_ge(vec, c.seen(vec))
                        v.scalar_tensor_tensor(out=cbuf[:, m, :], in0=gex[:, m, 2:GEX],
                                                        scalar=col(par, PAR["fw"] + 2 * FT + t), in1=cbuf[:, m, :],
                                                        op0=ALU.mult, op1=ALU.add).then_inc(
                                                            conv3_full, c.up(conv3_full))

                def history(i):
                    for m in range(2):
                        ins = v.tensor_copy(gex[:, m, 2 + SEQ:4 + SEQ], row(fhist, 2 * i + m, 0, 2))
                        ins.then_inc(gex_full, c.up(gex_full))

                def f_rows(i):
                    for b in range(4):
                        m, h = b % 2, b // 2
                        dve.wait_ge(acc_full[b], c.take(acc_full[b]))
                        if b < 2:
                            dve.wait_ge(fgelu_full, c.take(fgelu_full))
                            v.tensor_tensor(tmp[:, b, :], ps[b][:, 0:HALF], cbuf[:, m, 0:HALF], ALU.mult).then_inc(
                                acc_free[b], c.up(acc_free[b]))
                        else:
                            v.tensor_tensor(tmp[:, b, 0:BP], ps[b][:, 0:BP], cbuf[:, m, HALF:SEQ], ALU.mult).then_inc(
                                vec, c.up(vec))
                            v.tensor_tensor(tmp[:, b, BP:HALF], ps[b][:, BP:HALF], cbuf[:, m, SEQ + 2:GEX - 2],
                                                     ALU.mult).then_inc(acc_free[b], c.up(acc_free[b]))
                    for b in range(4):
                        dve.wait_ge(f_hi, c.take(f_hi))
                        v.tensor_tensor(row(fll[b // 2], 2 * i + b % 2, 0, HALF), tmp[:, b, :],
                                                 row(fhh[b // 2], 2 * i + b % 2, 0, HALF).bitcast(F32),
                                                 ALU.subtract).then_inc(f_ready, c.up(f_ready))

                history(0)
                conv_close(0)
                f_rows(0)
                with dve.Fori(0, 10) as i, c.loop("up", 10, i):
                    history(i + 1)
                    conv_close(i + 1)
                    f_rows(i + 1)

                with dve.Fori(0, 2) as i, c.loop("down0", 2, i):
                    for b in range(4):
                        residual(4 * i + b, b, 0)
                dve.wait_ge(acc_free[3], c.seen(acc_free[3]))
                ln_open(KT, x0)
                ln_centre(KT, x0)
                ln_squares(KT, sq)
                ln_norm_(KT, x0, sq)
                ln_value("ln2_g", "ln2_b", 0)
                ln_lo(0)
                for i in range(2):
                    for b in range(4):
                        residual(4 * i + b, b, 1)
                dve.wait_ge(acc_free[3], c.seen(acc_free[3]))
                ln_open(KT, x1)
                ln_centre(KT, x1)
                ln_squares(KT, sq)
                ln_norm_(KT, x1, sq)
                ln_value("ln2_g", "ln2_b", 1)
                ln_lo(1)
                dve.wait_ge(ffn_stored, c.take(ffn_stored, 16))
                dve.wait_ge(x_ready[1], c.seen(x_ready[1]))
                v.memset(st0[:, 0:1], 0.0).then_inc(layer_done, c.up(layer_done))

        @block.tensor
        def _(pe):
            c = Count("pe", adds)
            mm = pe.matmul
            turn = [0]
            turned_by = [None]
            small_by = [None]
            pe.wait_ge(consts, 19)

            def arrived():
                s = turn[0] % 2
                turn[0] += 1
                pe.wait_ge(lo_full[s], c.take(lo_full[s]))
                return s

            def three(out, s, at, xs, start, stop):
                a, b = wh[s][:, at:at + P], wl[s][:, at:at + P]
                mm(out, a, xs[0], start=start, stop=False)
                mm(out, a, xs[1], start=False, stop=False)
                return mm(out, b, xs[0], start=False, stop=stop)

            def unit(s, b, m, xs, nk, each=None, mid=None):
                pe.wait_ge(acc_free[b], c.prev(acc_free[b]))
                for t in range(nk):
                    if each:
                        each(t)
                    last = three(ps[b][:, 0:HALF], s, t * 256 + m * P, [x[:, t, dcol(b // 2)] for x in xs],
                                 t == 0, t == nk - 1)
                    if mid and t == nk // 2 - 1:
                        mid()
                last.then_inc(acc_full[b], c.up(acc_full[b]))

            def chunk(xs=(xh, xl), nk=KT, first=None, mid=None, end=None):
                s = arrived()
                for b in range(4):
                    unit(s, b, b % 2, xs, nk, first and (lambda t, b=b: first(t, b)), mid and (lambda b=b: mid(b)))
                    if end:
                        end(b)

            def half_chunk(h, banks, src, w=256):
                s = arrived()
                for m, b in enumerate(banks):
                    pe.wait_ge(acc_free[b], c.prev(acc_free[b]))
                    for t in range(KT):
                        last = three(ps[b][:, 0:HALF], s, t * w + m * P, [x[:, t, dcol(h)] for x in src],
                                     t == 0, t == KT - 1)
                    last.then_inc(acc_full[b], c.up(acc_full[b]))

            def ln_mean_(ones):
                pe.wait_ge(ln_sum, c.take(ln_sum))
                mm(bo[:, 0:HALF], ones[:, :], st0[:, :], start=True, stop=True).then_inc(ln_mean, c.up(ln_mean))

            def ln_var_(ones):
                pe.wait_ge(ln_ssum, c.take(ln_ssum))
                mm(bo[:, 0:HALF], ones[:, :], st0[:, :], start=True, stop=True).then_inc(ln_var, c.up(ln_var))

            def scores(u, b):
                ht, i = u // 4, u % 4
                rows = slice(DH * b, DH * b + DH)
                pe.wait_ge(sig_full[b], c.prev(sig_full[b]))
                mm(bs[b][:, 0:(i + 1) * P], q[rows, ht, i * P:(i + 1) * P], k[rows, ht, 0:(i + 1) * P],
                            start=True, stop=True).then_inc(s_full[b], c.up(s_full[b]))

            def turn_bank():
                if turned_by[0] is not None:
                    pe.wait_ge(turned_by[0], c.seen(turned_by[0]))

            def turns(u, b):
                pe.wait_ge(at_full[b], c.take(at_full[b]))
                turn_bank()
                for kb in range(u % 4 + 1):
                    last = pe.transpose(bt[:, kb * P:(kb + 1) * P], beta[b][:, kb * P:(kb + 1) * P], ident[:, :])
                last.then_inc(t_full, c.up(t_full))
                c.skip(att_full[b])
                turned_by[0] = att_full[b]

            def values(u, b):
                ht, i = u // 4, u % 4
                pe.wait_ge(att_full[b], c.seen(att_full[b]))
                if b == 0:
                    pe.wait_ge(o_hi, c.prev(o_hi))
                for kb in range(i + 1):
                    last = mm(bo[DH * b:DH * b + DH, 0:P], vtok[:, kb, (2 * ht + b) * DH:(2 * ht + b + 1) * DH],
                              att[b][:, kb * P:(kb + 1) * P], start=kb == 0, stop=kb == i)
                if b == 1:
                    last.then_inc(o_full, c.up(o_full))

            def step(n, end):
                if not end:
                    if 1 <= n <= STEPS:
                        turns(n - 1, 0)
                    if 2 <= n <= STEPS + 1:
                        values(n - 2, 1)
                    if n < STEPS:
                        scores(n, 0)
                else:
                    if 1 <= n <= STEPS:
                        values(n - 1, 0)
                        turns(n - 1, 1)
                    if n < STEPS:
                        scores(n, 1)

            def sample_scores(s):
                rows = slice(DH * s, DH * s + DH)
                for b, (keys, n) in enumerate(((kc[rows, :, :], PAST), (k[rows, :, SEQ:T], DEC))):
                    pe.wait_ge(sig_full[b], c.prev(sig_full[b]))
                    pe.sem_inc(passed, 1)
                    for ht in range(CT):
                        last = mm(bs[b][DEC * ht:DEC * ht + DEC, 0:n], q[rows, ht, SEQ:T], keys[:, ht, :],
                                  start=True, stop=True)
                    last.then_inc(s_full[b], c.up(s_full[b]))

            def sample_turns(s):
                pe.wait_ge(at_full[s], c.take(at_full[s]))
                turn_bank()
                for kb in range(4):
                    last = pe.transpose(bt[:, kb * P:(kb + 1) * P], beta[s][:, kb * P:(kb + 1) * P], ident[:, :])
                last.then_inc(t_full, c.up(t_full))
                c.skip(att_full[s])
                pe.wait_ge(att_full[s], c.seen(att_full[s]))
                pe.transpose(bt[0:DEC, 0:P], beta[s][:, PAST:PAST + DEC], ident[:, :]).then_inc(t_full, c.up(t_full))
                c.skip(att_full[s])
                turned_by[0] = att_full[s]

            def sample_values(s):
                pe.wait_ge(att_full[s], c.seen(att_full[s]))
                if s == 0:
                    pe.wait_ge(o_hi, c.prev(o_hi))
                for ht in range(CT):
                    h = 2 * ht + s
                    out = bo[DH * s:DH * s + DH, ht * DEC:(ht + 1) * DEC]
                    for kb in range(4):
                        mm(out, vc[:, kb, h * DH:(h + 1) * DH], att[s][:, kb * P + ht * DEC:kb * P + (ht + 1) * DEC],
                           start=kb == 0, stop=False)
                    last = mm(out, vtok[0:DEC, 4, h * DH:(h + 1) * DH],
                              att[s][0:DEC, PAST + ht * DEC:PAST + (ht + 1) * DEC], start=False, stop=True)
                if s == 1:
                    last.then_inc(o_full, c.up(o_full))

            def turn_tokens(src, t, sig_to, by):
                n = P if t < 4 else DEC
                turn_bank()
                for m in range(CT):
                    last = pe.transpose(bt[0:n, m * P:(m + 1) * P], src[:, m, t * P:t * P + n], ident[:, :])
                last.then_inc(sig_to, c.up(sig_to))
                c.skip(by)
                turned_by[0] = by

            with pe.Fori(0, DEPTH) as r, c.loop("layer", DEPTH, r):
                turned_by[0] = None

                def x_tiles(t, b):
                    if b in (0, 2):
                        pe.wait_ge(x_ready[b // 2], c.take(x_ready[b // 2]))

                chunk(first=x_tiles)
                chunk()

                def turn_v(n):
                    def after(b):
                        t = 4 * n + b
                        if t < 5:
                            if t == 0:
                                for bb in range(4):
                                    pe.wait_ge(acc_free[bb], c.seen(acc_free[bb], 1))
                            turn_tokens(vfm, t, v_turned, vtok_full)
                    return after

                chunk()
                chunk(end=turn_v(0))
                chunk(end=turn_v(1))
                chunk()
                pe.wait_ge(small_full, c.take(small_full, 160))
                for b in range(4):
                    pe.wait_ge(acc_free[b], c.seen(acc_free[b]))
                for n in range(4):
                    chunk(mid=lambda b, n=n: step(4 * n + b, False), end=lambda b, n=n: step(4 * n + b, True))

                def mid(b):
                    step(STEPS + b, False)
                    if b < 2:
                        sample_scores(b)
                    if 1 <= b < 3:
                        sample_turns(b - 1)

                def end(b):
                    step(STEPS + b, True)
                    if 2 <= b:
                        sample_values(b - 2)

                chunk(mid=mid, end=end)
                chunk()

                def turn_gv(n):
                    def after(b):
                        t = 4 * n + b
                        if t == 0:
                            pe.wait_ge(gelu_v, c.take(gelu_v))
                            for bb in range(4):
                                pe.wait_ge(acc_free[bb], c.seen(acc_free[bb], 1 if bb == 0 else 0))
                        if t < 5:
                            turn_tokens(gv, t, tok_turned, tok_full)
                    return after

                chunk(end=turn_gv(0))
                chunk(end=turn_gv(1))

                def mix():
                    pe.wait_ge(ntok_full, c.take(ntok_full))
                    pe.wait_ge(sgu_masked, c.take(sgu_masked))
                    turn_bank()
                    for g_ in range(CT):
                        if g_ > 1:
                            pe.wait_ge(mixed_used, c.seen(mixed_used, CT - g_ + 1))
                        if g_ == 0:
                            for gg in range(CT):
                                last = mm(bt[:, gg * DEC:(gg + 1) * DEC], ntok[0:DEC, 4, gg * P:(gg + 1) * P],
                                          wsgu[0:DEC, gg, 0:DEC], start=True, stop=True)
                            last.then_inc(mixed, c.up(mixed))
                            c.skip(mixed_used, CT)
                        for t in range(4):
                            last = mm(bs[g_ % 2][:, t * P:(t + 1) * P], ntok[:, t, g_ * P:(g_ + 1) * P], wsgu[:, g_, :],
                                      start=True, stop=True)
                        last.then_inc(mixed, c.up(mixed))
                    turned_by[0] = mixed_used

                ybs = dict(xs=yb, nk=CT)
                chunk()
                mix()
                c.skip(yb_full, CT)
                chunk(**ybs, first=lambda t, b: pe.wait_ge(yb_full, c.seen(yb_full, CT - 1 - t)) if b == 0 else None)
                with pe.Fori(0, 3) as r, c.loop("branch0", 3, r):
                    chunk()
                    chunk(**ybs)
                c.skip(yc_full, STEPS + 1)
                chunk()
                pe.wait_ge(yc_full, c.seen(yc_full))
                chunk(xs=yc, nk=CT)
                with pe.Fori(0, 3) as r, c.loop("branch1", 3, r):
                    chunk()
                    chunk(xs=yc, nk=CT)

                chunk(end=lambda b: (ln_mean_, ln_var_)[b % 2](mean_c))

                def ya_tiles(t, b):
                    if b in (0, 2):
                        pe.wait_ge(ya_full, c.take(ya_full))
                chunk(xs=ya, nk=CT, first=ya_tiles)
                with pe.Fori(0, 3) as r, c.loop("branch2", 3, r):
                    chunk()
                    chunk(xs=ya, nk=CT)

                pe.wait_ge(m_ready[0], c.take(m_ready[0], KT))
                pe.sem_inc(passed, 1)
                with pe.Fori(0, 2) as r, c.loop("out0", 2, r):
                    half_chunk(0, (0, 1), (mh, ml))
                    half_chunk(0, (2, 3), (mh, ml))
                pe.wait_ge(m_ready[1], c.take(m_ready[1], KT))
                for i in range(2):
                    half_chunk(1, (0, 1), (mh, ml))
                    if i == 0:
                        ln_mean_(mean_d)
                    half_chunk(1, (2, 3), (mh, ml))
                    if i == 0:
                        ln_var_(mean_d)

                s0 = arrived()
                unit(s0, 0, 0, (xh, xl), KT, lambda t: pe.wait_ge(x_ready[0], c.take(x_ready[0])))
                unit(s0, 1, 1, (xh, xl), KT)
                ln_mean_(mean_d)
                s1 = arrived()
                unit(s1, 0, 0, (xh, xl), KT)
                ln_var_(mean_d)
                unit(s1, 1, 1, (xh, xl), KT)
                unit(s0, 2, 0, (xh, xl), KT, lambda t: pe.wait_ge(x_ready[1], c.take(x_ready[1])))
                unit(s0, 3, 1, (xh, xl), KT)
                unit(s1, 2, 0, (xh, xl), KT)
                unit(s1, 3, 1, (xh, xl), KT)
                with pe.Fori(0, 10) as r, c.loop("up", 10, r):
                    chunk()
                    chunk()

                def down(h, middle=None):
                    at = 0
                    for j, kn in enumerate(KGROUPS):
                        s = arrived()
                        for b in range(4):
                            if j == 0:
                                pe.wait_ge(acc_free[b], c.prev(acc_free[b]))
                            for t in range(kn):
                                last = three(ps[b][:, 0:HALF], s, t * 512 + b * P,
                                             [f[h][:, at + t, :] for f in (fhh, fll)],
                                             j == 0 and t == 0, j == len(KGROUPS) - 1 and t == kn - 1)
                            if j == len(KGROUPS) - 1:
                                last.then_inc(acc_full[b], c.up(acc_full[b]))
                        if j < len(KGROUPS) - 1:
                            last.then_inc(part_used[s], c.up(part_used[s]))
                        at += kn
                        if middle and j < 2:
                            middle[j]()

                pe.wait_ge(f_ready, c.take(f_ready, 4 * 11))
                pe.sem_inc(passed, 1)
                with pe.Fori(0, 2) as r, c.loop("down0", 2, r):
                    down(0)
                down(1, (lambda: ln_mean_(mean_d), lambda: ln_var_(mean_d)))
                down(1)
                ln_mean_(mean_d)
                ln_var_(mean_d)


def acc_view(acc, h):
    return acc[:, :, h * HALF:(h + 1) * HALF]


def kernel(**inputs):
    import numpy as np
    import concourse.bacc as bacc
    from concourse.bass_utils import run_bass_kernel_spmd

    a = {n: np.asarray(v) for n, v in inputs.items()}

    def cols(w, n):
        L, K, C = w.shape
        return w.reshape(L, K // P, P, C // n, n).transpose(0, 3, 2, 1, 4).reshape(L, C // n, P, (K // P) * n)

    def chan(v, n):
        return v.reshape(DEPTH, -1, n, P).transpose(0, 3, 1, 2).reshape(DEPTH, P, -1)

    def feat(v):
        L, r, ch = v.shape
        return v.reshape(L, r, ch // P, P).transpose(0, 3, 2, 1)

    arrays = {
        "x_in": feat(np.concatenate([a["x_prompt"], a["x_sample"]], axis=1))[0],
        "win": cols(a["w_in"], 256).reshape(-1, P, CHUNK),
        "wbr": cols(a["w_branch"].reshape(DEPTH * 3, CH, D), 256).reshape(-1, P, CHUNK // 2),
        "wout": cols(a["w_out"], 256).reshape(-1, P, CHUNK),
        "wup": cols(a["w_up"], 256).reshape(-1, P, CHUNK),
        "wdn": cols(a["w_down"], 512).reshape(-1, P, FT * 512),
        "par_in": np.concatenate([chan(a["b_gate"], KT), chan(a["conv_w"], CT), chan(a["conv_b"], CT),
                                  chan(a["conv_ln_g"], CT), chan(a["conv_ln_b"], CT), chan(a["ln1_g"], KT),
                                  chan(a["ln1_b"], KT), chan(a["ln2_g"], KT), chan(a["ln2_b"], KT),
                                  chan(a["ffn_conv_w"], FT), chan(a["ffn_conv_b"], FT)], axis=2),
        "bc_in": np.broadcast_to(np.stack([a["sgu_ln_g"], a["sgu_ln_b"], a["sgu_b"].reshape(DEPTH, CH)], axis=1)
                                 .reshape(DEPTH, 1, 3 * CH), (DEPTH, P, 3 * CH)),
        "sguw_in": a["sgu_w"].transpose(0, 3, 1, 2).reshape(DEPTH, P, CH),
        "kc_in": feat(a["cache_sb_k"].reshape(DEPTH, PAST, CH)).reshape(DEPTH, P, CT * PAST),
        "vc_in": a["cache_sb_v"].reshape(DEPTH, 4, P, CH).transpose(0, 2, 1, 3).reshape(DEPTH, P, 4 * CH),
        "gh_in": a["state_conv_glu"].reshape(DEPTH, HIST, CT, P).transpose(0, 2, 3, 1).reshape(DEPTH * CT, P, HIST),
        "fh_in": feat(a["state_ffn_conv"].reshape(DEPTH, 2, FF)).reshape(DEPTH, P, FT * 2),
    }
    arrays = {n: np.ascontiguousarray(v) for n, v in arrays.items()}
    outs = {"y_out": (P, KT, T), "k_out": (DEPTH, P, CT * T), "v_out": (DEPTH, P, CT * T),
            "glu_out": (DEPTH * CT * 2, P, HIST), "ffn_out": (DEPTH, P, FT * 4), "sgu_out": (DEPTH, DEC, CH)}

    adds = {}
    for _ in range(2):
        nc = bacc.Bacc("TRN2", target_bir_lowering=False, num_devices=1, dynamic_dma_scratch_size=1024)
        ins = [nc.dram_tensor(n, v.shape, F32, kind="ExternalInput").ap() for n, v in arrays.items()]
        out = [nc.dram_tensor(n, s, F32, kind="ExternalOutput").ap() for n, s in outs.items()]
        trunk(nc, adds, *ins, *out)
    r = run_bass_kernel_spmd(nc, [arrays], core_ids=[0]).results[0]

    def rows(v):
        v = np.moveaxis(v, -1, -3)
        v = np.swapaxes(v, -1, -2)
        return v.reshape(*v.shape[:-2], -1)

    y = rows(r["y_out"])
    kk = rows(r["k_out"].reshape(DEPTH, P, CT, T)).reshape(DEPTH, 1, T, 8, DH)
    vv = rows(r["v_out"].reshape(DEPTH, P, CT, T)).reshape(DEPTH, 1, T, 8, DH)
    gl = r["glu_out"].reshape(DEPTH, CT, 2, P, HIST).transpose(0, 2, 4, 1, 3).reshape(DEPTH, 2, 1, HIST, CH)
    ff = r["ffn_out"].reshape(DEPTH, P, FT, 2, 2).transpose(0, 3, 4, 2, 1).reshape(DEPTH, 2, 1, 2, FF)
    res = (y[None, :SEQ], y[None, SEQ:], kk[:, :, :SEQ], vv[:, :, :SEQ], gl[:, 0], ff[:, 0],
           kk[:, :, SEQ:], vv[:, :, SEQ:], gl[:, 1], ff[:, 1], r["sgu_out"].reshape(DEPTH, 1, DEC, CH))
    return tuple(np.ascontiguousarray(v) for v in res)
```

```python
from contextlib import ExitStack, contextmanager

import concourse.bass as bass
from concourse import mybir

F32 = mybir.dt.float32
F32R = mybir.dt.float32r
ALU = mybir.AluOpType
ACT = mybir.ActivationFunctionType
AX_X = mybir.AxisListType.X

P = 128
D = 1024
SEQ = 512
DEC = 32
T = SEQ + DEC
HALF = T // 2
BP = SEQ - HALF
KT = D // P
DEPTH = 2
CH = 512
CT = CH // P
WID = 31
HIST = WID - 1
PAST = 512
DH = 64
FF = 2816
FT = FF // P
GT = HIST + SEQ + HIST + DEC
CV = GT - HIST
SCOL = SEQ + HIST
GEX = 2 + SEQ + 2 + DEC
ALPHA = (2 * DEPTH) ** 0.25
EPS = 1e-5
CHUNK = 2048
WIN_CHUNKS = 26
UP_CHUNKS = 22
T4 = CT * T * 4

PAR = {}
_at = 0
for _n, _w in (("b_gate", 24), ("conv_w", WID * CT), ("conv_b", CT), ("conv_g", CT), ("conv_bb", CT),
               ("ln1_g", KT), ("ln1_b", KT), ("ln2_g", KT), ("ln2_b", KT), ("fw", 3 * FT), ("fb", FT)):
    PAR[_n] = _at
    _at += _w
NPAR = _at

UV_TAPS, B_TAPS, C_FIRST, C_TAPS = (2, 2, 0, 2), 5, 5, 2
KGROUPS = (4, 2, 4, 4, 4, 4)
assert sum(KGROUPS) == FT
STARTS_AT_1 = ("lo_full", "rest_full", "acc_free", "acc_full", "part_used", "sig_full", "o_hi", "layer_done", "m_sum", "vec",
               "yc_full", "att_full", "mixed_used")
assert sum(UV_TAPS) + 3 * B_TAPS + C_FIRST + 2 * C_TAPS == WID - 1


class Count:

    def __init__(self, name, adds):
        self.name, self.adds = name, adds
        self.n, self.loops = {}, []

    @staticmethod
    def starts_at(sem):
        return int(sem.name.rstrip("0123456789") in STARTS_AT_1)

    def seen(self, sem, back=0):
        v = self.n.get(sem.name, 0) - back + self.starts_at(sem)
        for i, key in self.loops:
            step = self.adds.get((self.name, key, sem.name), 0)
            if step:
                v = i * step + v
        return v

    def up(self, sem, by=1):
        self.n[sem.name] = self.n.get(sem.name, 0) + by
        return by

    def take(self, sem, by=1):
        self.up(sem, by)
        return self.seen(sem)

    def skip(self, sem, by=1):
        self.up(sem, by)

    def prev(self, sem):
        v = self.seen(sem)
        self.up(sem)
        return v

    @contextmanager
    def loop(self, key, n, i):
        start = dict(self.n)
        self.loops.append((i, key))
        yield
        self.loops.pop()
        for s, v in list(self.n.items()):
            add = v - start.get(s, 0)
            self.adds[(self.name, key, s)] = add
            self.n[s] = start.get(s, 0) + n * add


def row(tile, idx, a, b):
    if isinstance(idx, int):
        return tile[:, idx, a:b]
    return tile[:, bass.ds(idx, 1), a:b].rearrange("p o n -> p (o n)")


def col(tile, idx):
    if isinstance(idx, int):
        return tile[:, idx:idx + 1]
    return tile[:, bass.ds(idx, 1)]


def trunk(nc, adds, x_in, win, wbr, wout, wup, wdn, par_in, bc_in, sguw_in, kc_in, vc_in, gh_in, fh_in,
          y_out, k_out, v_out, glu_out, ffn_out, sgu_out):
    with ExitStack() as ctx:
        sems = {}

        def sem(name):
            sems[name] = ctx.enter_context(nc.semaphore(name))
            return sems[name]

        top = [(nc.sbuf_base + 31) // 32 * 32]

        def sb(name, shape, dt=F32, at=None):
            size = 4
            for s in shape[1:]:
                size *= s
            off = at
            if at is None:
                off = top[0]
                top[0] += (size + 31) // 32 * 32
            return nc.alloc_sbuf_tensor_at(name, shape, dt, offset=off)

        xT = sb("xT", [P, KT, T])
        xh = sb("xh", [P, KT, T], F32R)
        xl = sb("xl", [P, KT, T], F32R)
        raw = [sb(f"raw{s}", [P, CHUNK]) for s in range(2)]
        wh = [sb(f"wh{s}", [P, CHUNK], F32R) for s in range(2)]
        wl = [sb(f"wl{s}", [P, CHUNK], F32R) for s in range(2)]
        ident = sb("ident", [P, P])
        mean_d = sb("mean_d", [P, P])
        mean_c = sb("mean_c", [P, P])
        past1 = sb("past1", [P, P])
        past0 = sb("past0", [P, P])
        spast1 = sb("spast1", [P, DEC])
        spast0 = sb("spast0", [P, DEC])
        zero = sb("zero", [P, 1])
        eps = sb("eps", [P, 1])
        par = sb("par", [P, NPAR])
        st0 = sb("st0", [P, HALF])
        st1 = sb("st1", [P, HALF])
        st2 = sb("st2", [P, HALF])
        fst = sb("fst", [P, FT, 4])
        fhist = sb("fhist", [P, FT, 2])
        tmp = sb("tmp", [P, 4, HALF])
        wsgu = sb("wsgu", [P, CT, P])
        bc = sb("bc", [P, 3, CH])
        bnst = sb("bnst", [P, 5, 6])
        mv = sb("mv", [P, 5, 2])
        rs = sb("rs", [P, 2, 5])
        otmp = sb("otmp", [P, P])
        gex = sb("gex", [P, 2, GEX])
        cbuf = sb("cbuf", [P, 2, GEX - 2])
        F = top[0]
        assert F + 11 * T4 <= nc.sbuf_usable_end, F + 11 * T4
        fhh = [sb(f"fhh{h}", [P, FT, HALF], F32R, at=F + h * 2 * FT * HALF * 4) for h in range(2)]
        fll = [sb(f"fll{h}", [P, FT, HALF], F32R, at=F + (2 * h + 1) * FT * HALF * 4) for h in range(2)]
        yb = [sb(n, [P, CT, T], F32R, at=F + i * T4) for i, n in enumerate(("ybh", "ybl"))]
        q = sb("q", [P, CT, T], at=F)
        k = sb("k", [P, CT, T], at=F + T4)
        mh = sb("mh", [P, KT, T], F32R, at=F)
        yc = [sb(n, [P, CT, T], F32R, at=F + (2 + i) * T4) for i, n in enumerate(("ych", "ycl"))]
        ml = sb("ml", [P, KT, T], F32R, at=F + 2 * T4)
        merged = sb("merged", [P, KT, T], at=F + 4 * T4)
        kc = sb("kc", [P, CT, PAST], at=F + 4 * T4)
        vc = sb("vc", [P, CT, CH], at=F + 4 * T4 + CT * PAST * 4)
        gu = sb("gu", [P, CT, T], at=F + 4 * T4)
        sq = sb("sq", [P, KT, HALF], at=F + 39168)
        vtok = sb("vtok", [P, 5, CH], at=F + 6 * T4)
        ntok = sb("ntok", [P, 5, CH], at=F + 6 * T4)
        ya = [sb(n, [P, CT, T], F32R, at=F + (6 + i) * T4) for i, n in enumerate(("yah", "yal"))]
        vfm = sb("vfm", [P, CT, T], at=F + 62464)
        gv = sb("gv", [P, CT, T], at=F + 62464)
        glu = sb("glu", [P, CT, GT], at=F + 71168)
        acc = sb("acc", [P, CT, CV], at=F + 80832)
        keep = [sb(f"keep{i}", [P, T + 4], at=F + 80832 + i * 6976) for i in range(2)]
        beta = [sb(f"beta{i}", [P, T], at=F + 80832 + i * 6976 + 2208) for i in range(2)]
        att = [sb(f"att{i}", [P, 5 * P], at=F + 80832 + i * 6976 + 2208 + 2176) for i in range(2)]
        sqc = sb("sqc", [P, CT, HALF], at=F + 90016)

        ps = [ctx.enter_context(nc.psum_tensor(f"acc{b}", [P, 512], F32)) for b in range(4)]
        bs = [ctx.enter_context(nc.psum_tensor(f"score{b}", [P, 512], F32)) for b in range(2)]
        bt = ctx.enter_context(nc.psum_tensor("turned", [P, 512], F32))
        bo = ctx.enter_context(nc.psum_tensor("small", [P, 512], F32))

        x_loaded = [sem(f"x_loaded{h}") for h in range(2)]
        x_hi = sem("x_hi")
        consts = sem("consts")
        passed = sem("passed")
        raw_full = [sem(f"raw_full{s}") for s in range(2)]
        hi_full = [sem(f"hi_full{s}") for s in range(2)]
        lo_full = [sem(f"lo_full{s}") for s in range(2)]
        hi_rest = [sem(f"hi_rest{s}") for s in range(2)]
        rest_full = [sem(f"rest_full{s}") for s in range(2)]
        part_used = [sem(f"part_used{s}") for s in range(2)]
        acc_full = [sem(f"acc_full{b}") for b in range(4)]
        acc_free = [sem(f"acc_free{b}") for b in range(4)]
        x_ready = [sem(f"x_ready{h}") for h in range(2)]
        small_full = sem("small_full")
        layer_done = sem("layer_done")
        sgu_masked = sem("sgu_masked")
        kv_stored = sem("kv_stored")
        v_turned = sem("v_turned")
        vtok_full = sem("vtok_full")
        s_full = [sem(f"s_full{i}") for i in range(2)]
        sig_full = [sem(f"sig_full{i}") for i in range(2)]
        at_full = [sem(f"at_full{i}") for i in range(2)]
        t_full = sem("t_full")
        att_full = [sem(f"att_full{i}") for i in range(2)]
        o_full = sem("o_full")
        o_hi = sem("o_hi")
        yc_full = sem("yc_full")
        vec = sem("vec")
        glu_full = sem("glu_full")
        glu_stored = sem("glu_stored")
        gelu_v = sem("gelu_v")
        gelu_u = sem("gelu_u")
        tok_turned = sem("tok_turned")
        tok_full = sem("tok_full")
        tok_var = sem("tok_var")
        tok_std = sem("tok_std")
        ntok_full = sem("ntok_full")
        sgu_stored = sem("sgu_stored")
        mixed = sem("mixed")
        mixed_used = sem("mixed_used")
        yb_sum = sem("yb_sum")
        yb_hi = sem("yb_hi")
        yb_full = sem("yb_full")
        ln_sum = sem("ln_sum")
        ln_mean = sem("ln_mean")
        ln_cent = sem("ln_cent")
        ln_sq = sem("ln_sq")
        ln_ssum = sem("ln_ssum")
        ln_var = sem("ln_var")
        ln_std = sem("ln_std")
        ln_norm = sem("ln_norm")
        ln_hi = sem("ln_hi")
        ya_full = sem("ya_full")
        m_sum = sem("m_sum")
        m_hi = sem("m_hi")
        m_ready = [sem(f"m_ready{h}") for h in range(2)]
        gex_full = sem("gex_full")
        tap0_full = sem("tap0_full")
        conv3_full = sem("conv3_full")
        fgelu_full = sem("fgelu_full")
        f_hi = sem("f_hi")
        f_ready = sem("f_ready")
        ffn_stored = sem("ffn_stored")
        stored = sem("stored")

        QKV = (12, 13, 8, 9, 10, 11)
        GLU = (2, 0, 3, 1)
        UV = (6, 7, 4, 5)
        GATE = 14
        BRANCHES = (1, 2, 0)
        STEPS = 16

        def dcol(h):
            return slice(h * HALF, (h + 1) * HALF)

        block = ctx.enter_context(nc.Block())

        @block.sync
        def _(sp):
            c = Count("sp", adds)
            for s in sems.values():
                if c.starts_at(s):
                    sp.sem_inc(s, 1)
            turn = [0]

            def chunk(src, size=CHUNK, parts=1):
                s = turn[0] % 2
                turn[0] += 1
                sp.wait_ge(lo_full[s], c.prev(lo_full[s]))
                sp.sem_inc(passed, 1)
                sp.wait_ge(rest_full[s], c.seen(rest_full[s]))
                if parts == 2:
                    c.skip(rest_full[s])
                sp.dma_start(raw[s][:, 0:size], src).then_inc(raw_full[s], c.up(raw_full[s], 16))

            def flat(ap):
                return ap.rearrange("a p n -> (a p) n")

            with sp.Fori(0, DEPTH) as l, c.loop("layer", DEPTH, l):
                def w_in(i, parts=1):
                    chunk(flat(win[bass.ds(l * WIN_CHUNKS + i, 1)]), parts=parts)

                for n in range(4):
                    w_in(QKV[n])
                sp.wait_ge(layer_done, c.prev(layer_done))
                for dst, src in ((par, par_in), (bc, bc_in), (wsgu, sguw_in), (kc, kc_in), (vc, vc_in),
                                 (fhist, fh_in)):
                    flat_dst = dst[:, :] if len(dst.shape) == 2 else dst[:, :, :].rearrange("p a n -> p (a n)")
                    sp.dma_start(flat_dst, flat(src[bass.ds(l, 1)])).then_inc(small_full, c.up(small_full, 16))
                for m in range(CT):
                    sp.dma_start(glu[:, m, SCOL:SCOL + HIST],
                                          flat(gh_in[bass.ds(l * CT + m, 1)])).then_inc(
                                              small_full, c.up(small_full, 16))
                for n in range(4, 6):
                    w_in(QKV[n])
                for n in range(4):
                    w_in(GLU[n])
                w_in(UV[0])
                for n in range(1, 3):
                    w_in(UV[n])
                sp.wait_ge(glu_full, c.take(glu_full, CT))
                for m in range(CT):
                    for j, a in enumerate((SEQ, GT - HIST)):
                        sp.dma_start(flat(glu_out[bass.ds(l * 2 * CT + 2 * m + j, 1)]), glu[:, m, a:a + HIST]).then_inc(
                            glu_stored, c.up(glu_stored, 16))
                w_in(UV[3])
                for n, b in enumerate(BRANCHES):
                    def pair(i, parts=2, b=b):
                        w_in(GATE + 4 * b + i, parts)
                        chunk(flat(wbr[bass.ds(l * 12 + 4 * b + i, 1)]), CHUNK // 2)
                    pair(0, 1 if n == 0 else 2)
                    if n == 0:
                        sp.wait_ge(ntok_full, c.take(ntok_full))
                        sp.dma_start(flat(sgu_out[bass.ds(l, 1)]), ntok[0:DEC, 4, :]).then_inc(
                            sgu_stored, c.up(sgu_stored, 16))
                    with sp.Fori(0, 3) as i, c.loop(f"branch{n}", 3, i):
                        pair(i + 1)
                for h in range(2):
                    with sp.Fori(0, 2) as i, c.loop(f"out{h}", 2, i):
                        for j in range(2):
                            chunk(flat(wout[bass.ds(l * 4 + 2 * i + j, 1)]), parts=2)
                for j in range(2):
                    chunk(flat(wup[bass.ds(l * UP_CHUNKS + 11 * j, 1)]), parts=2 - j)
                with sp.Fori(0, 10) as i, c.loop("up", 10, i):
                    for j in range(2):
                        chunk(flat(wup[bass.ds(l * UP_CHUNKS + 11 * j + 1 + i, 1)]))
                for h in range(2):
                    if h == 1:
                        sp.wait_ge(conv3_full, c.take(conv3_full, FT))
                        sp.dma_start(flat(ffn_out[bass.ds(l, 1)]),
                                              fst[:, :, :].rearrange("p a n -> p (a n)")).then_inc(
                                                  ffn_stored, c.up(ffn_stored, 16))
                    with sp.Fori(0, 2) as i, c.loop(f"down{h}", 2, i):
                        at = 0
                        for kn in KGROUPS:
                            chunk(flat(wdn[bass.ds(l * 2 + i, 1), :, at * 512:(at + kn) * 512]), kn * 512,
                                  2 if at else 1)
                            at += kn
            chunk(win[0])
            chunk(win[0])
            for h in range(2):
                sp.wait_ge(x_ready[h], KT * (1 + 2 * DEPTH))
                sp.dma_start(y_out[:, :, dcol(h)], xT[:, :, dcol(h)]).then_inc(stored, 16)
            sp.wait_ge(stored, 32)
            sp.wait_ge(kv_stored, 32 * DEPTH)
            sp.wait_ge(glu_stored, 16 * 2 * CT * DEPTH)
            sp.wait_ge(sgu_stored, 16 * DEPTH)
            sp.wait_ge(ffn_stored, 16 * DEPTH)
            for s in range(2):
                sp.wait_ge(raw_full[s], c.n[raw_full[s].name])

        @block.gpsimd
        def _(pool):
            c = Count("pool", adds)
            g = nc.gpsimd
            for t, v in ((ident, 0.0), (past1, 1.0), (past0, 1.0), (spast1, 1.0), (spast0, 1.0),
                         (mean_d, 1.0 / D), (mean_c, 1.0 / CH), (zero, 0.0), (eps, EPS), (mv, 1.0)):
                ap = t[:, :] if len(t.shape) == 2 else t[:, :, :]
                g.memset(ap, v).then_inc(consts, c.up(consts))
            g.memset(gex[:, :, :], 0.0).then_inc(consts, c.up(consts))
            pool.wait_ge(consts, c.seen(consts))

            def select(t, op, base, fill, rows=slice(0, P), n=P):
                g.affine_select(out=t[rows, 0:n], in_=t[rows, 0:n], compare_op=op, fill=fill, base=base,
                                         pattern=[[-1, n]], channel_multiplier=1).then_inc(consts, c.up(consts))
                pool.wait_ge(consts, c.seen(consts))

            select(ident, ALU.not_equal, 0, 1.0)
            select(past0, ALU.is_gt, 0, 0.0)
            for j in range(4):
                select(spast0, ALU.is_gt, 0, 0.0, slice(32 * j, 32 * j + 32), DEC)
            pool.wait_ge(consts, c.seen(consts))
            g.tensor_tensor(past1[:, :], past1[:, :], past0[:, :], ALU.subtract).then_inc(consts, c.up(consts))
            g.tensor_tensor(spast1[:, :], spast1[:, :], spast0[:, :], ALU.subtract).then_inc(consts, c.up(consts))
            turn = [0]

            def chunk(size=CHUNK, parts=1):
                s = turn[0] % 2
                turn[0] += 1
                pool.wait_ge(hi_full[s], c.take(hi_full[s]))
                size //= parts
                g.tensor_tensor(wl[s][:, 0:size], raw[s][:, 0:size], wh[s][:, 0:size].bitcast(F32),
                                         ALU.subtract).then_inc(lo_full[s], c.up(lo_full[s]))

            with pool.Fori(0, DEPTH) as r, c.loop("layer", DEPTH, r):
                for n in range(4):
                    chunk()
                pool.wait_ge(small_full, c.take(small_full, 160))
                pool.sem_inc(passed, 1)
                g.affine_select(out=wsgu[:, :, :], in_=wsgu[:, :, :], compare_op=ALU.is_ge, fill=0.0, base=0,
                                         pattern=[[0, CT], [1, P]], channel_multiplier=-1).then_inc(
                                             sgu_masked, c.up(sgu_masked))
                for n in range(10):
                    chunk()
                for n in range(3):
                    chunk(parts=1 if n == 0 else 2)
                    chunk(CHUNK // 2)
                    with pool.Fori(0, 3) as r, c.loop(f"branch{n}", 3, r):
                        chunk(parts=2)
                        chunk(CHUNK // 2)
                for h in range(2):
                    with pool.Fori(0, 2) as r, c.loop(f"out{h}", 2, r):
                        chunk(parts=2)
                        chunk(parts=2)
                chunk(parts=2)
                chunk()
                with pool.Fori(0, 10) as r, c.loop("up", 10, r):
                    chunk()
                    chunk()
                for h in range(2):
                    with pool.Fori(0, 2) as r, c.loop(f"down{h}", 2, r):
                        for j, kn in enumerate(KGROUPS):
                            chunk(kn * 512, 2 if j else 1)

        @block.scalar
        def _(act):
            c = Count("act", adds)
            A = act.activation
            turn = [0]

            def hi(size=CHUNK, used=None, parts=1):
                s = turn[0] % 2
                turn[0] += 1
                if used is not None:
                    act.wait_ge(used, c.seen(used))
                act.wait_ge(raw_full[s], c.take(raw_full[s], 16))
                n = size // parts
                A(wh[s][:, 0:n], raw[s][:, 0:n], ACT.Copy).then_inc(hi_full[s], c.up(hi_full[s]))
                if parts == 2:
                    A(wh[s][:, n:size], raw[s][:, n:size], ACT.Copy).then_inc(hi_rest[s], c.up(hi_rest[s]))

            def ln_squares(nt, src, buf):
                for j in range(2):
                    act.wait_ge(ln_cent, c.take(ln_cent))
                    n = nt // 2
                    A(buf[:, j * n:(j + 1) * n, :], src[:, j * n:(j + 1) * n], ACT.Square).then_inc(ln_sq, c.up(ln_sq))

            def ln_root():
                act.wait_ge(ln_var, c.take(ln_var))
                A(st1[:, :], bo[:, 0:HALF], ACT.Sqrt, bias=eps[:, 0:1]).then_inc(ln_std, c.up(ln_std))

            def ln_write(nt, buf, dst, gname, bname, fn, h):
                for t in range(nt):
                    if t % (nt // 2) == 0:
                        act.wait_ge(ln_norm, c.take(ln_norm))
                    A(dst[:, t, dcol(h)], buf[:, t, :], fn, scale=col(par, PAR[gname] + t),
                               bias=col(par, PAR[bname] + t)).then_inc(ln_hi, c.up(ln_hi))

            def sig(b, n):
                act.wait_ge(s_full[b], c.take(s_full[b]))
                A(keep[b][:, 0:n], bs[b][:, 0:n], ACT.Sigmoid, scale=-DH ** -0.5)
                A(beta[b][:, 0:n], bs[b][:, 0:n], ACT.Sigmoid, scale=DH ** -0.5).then_inc(
                    sig_full[b], c.up(sig_full[b]))

            def turned(b, n):
                act.wait_ge(t_full, c.take(t_full))
                A(att[b][:, 0:n], bt[:, 0:n], ACT.Copy).then_inc(att_full[b], c.up(att_full[b]))

            def out_rows(u):
                act.wait_ge(o_full, c.take(o_full))
                ht, i = u // 4, u % 4
                A(yc[0][:, ht, i * P:(i + 1) * P], bo[:, 0:P], ACT.Copy)
                if u > 0:
                    act.wait_ge(yc_full, c.seen(yc_full))
                c.skip(yc_full)
                A(otmp[:, :], bo[:, 0:P], ACT.Copy).then_inc(o_hi, c.up(o_hi))

            def step(n, end):
                if not end:
                    if 1 <= n <= STEPS:
                        turned(0, ((n - 1) % 4 + 1) * P)
                    if 2 <= n <= STEPS + 1:
                        out_rows(n - 2)
                    if n < STEPS:
                        sig(0, (n % 4 + 1) * P)
                else:
                    if 1 <= n <= STEPS:
                        turned(1, ((n - 1) % 4 + 1) * P)
                    if n < STEPS:
                        sig(1, (n % 4 + 1) * P)

            def sample_sig(s):
                for b, (lo_, n) in enumerate(((0, PAST), (PAST, DEC))):
                    act.wait_ge(s_full[b], c.take(s_full[b]))
                    A(keep[s][:, lo_:lo_ + n], bs[b][:, 0:n], ACT.Sigmoid, scale=-DH ** -0.5)
                    A(beta[s][:, lo_:lo_ + n], bs[b][:, 0:n], ACT.Sigmoid, scale=DH ** -0.5).then_inc(
                        sig_full[b], c.up(sig_full[b]))

            def sample_turned(s):
                act.wait_ge(t_full, c.take(t_full))
                A(att[s][:, 0:PAST], bt[:, 0:PAST], ACT.Copy).then_inc(att_full[s], c.up(att_full[s]))
                act.wait_ge(t_full, c.take(t_full))
                A(att[s][0:DEC, PAST:PAST + P], bt[0:DEC, 0:P], ACT.Copy).then_inc(att_full[s], c.up(att_full[s]))

            def plain(dst, m, b, sig_to, fn=ACT.Copy):
                h = b // 2
                act.wait_ge(acc_full[b], c.take(acc_full[b]))
                A(dst[:, m, dcol(h)], ps[b][:, 0:HALF], fn).then_inc(acc_free[b], c.up(acc_free[b]))

            for h in range(2):
                act.dma_start(xT[:, :, dcol(h)], x_in[:, :, dcol(h)]).then_inc(x_loaded[h], 16)
            hi()
            hi()
            c.skip(ln_var)
            for h in range(2):
                act.wait_ge(x_loaded[h], 16)
                for t in range(KT):
                    A(xh[:, t, dcol(h)], xT[:, t, dcol(h)], ACT.Copy).then_inc(x_hi, c.up(x_hi))

            with act.Fori(0, DEPTH) as l, c.loop("layer", DEPTH, l):
                def plain_rows(n, b, h, bank=None):
                    dst, m = (vfm, q, k)[n // 2], 2 * (n % 2) + b % 2
                    act.wait_ge(acc_full[b], c.take(acc_full[b]))
                    A(dst[:, m, dcol(h)], (bank or ps[b])[:, 0:HALF], ACT.Copy).then_inc(acc_free[b], c.up(acc_free[b]))

                for b in range(4):
                    plain_rows(b // 2, b, 0)
                plain_rows(0, 0, 1, bs[0])
                plain_rows(0, 1, 1, bs[1])
                hi(used=acc_full[1])
                plain_rows(1, 2, 1)
                plain_rows(1, 3, 1)
                for n in range(2, 6):
                    hi(used=acc_full[3])
                    for b in range(4):
                        plain_rows(n, b, b // 2)
                for b in range(4):
                    act.wait_ge(acc_free[b], c.seen(acc_free[b]))
                for dst, src in ((k_out, k), (v_out, vfm)):
                    act.dma_start(dst[bass.ds(l, 1)].rearrange("a p n -> (a p) n"),
                                           src[:, :, :].rearrange("p a n -> p (a n)")).then_inc(
                                               kv_stored, c.up(kv_stored, 16))
                act.wait_ge(small_full, c.take(small_full, 160))
                for n in range(4):
                    hi(used=acc_full[3])
                    for b in range(4):
                        step(4 * n + b, False)
                        if n % 2 == 0:
                            act.wait_ge(acc_full[b], c.take(acc_full[b]))
                            A(tmp[:, b, :], ps[b][:, 0:HALF], ACT.Sigmoid).then_inc(acc_free[b], c.up(acc_free[b]))
                        else:
                            c.skip(acc_full[b])
                            c.skip(acc_free[b])
                        step(4 * n + b, True)
                act.wait_ge(kv_stored, c.seen(kv_stored))
                hi(used=acc_full[3])
                for b in range(4):
                    n = STEPS + b
                    step(n, False)
                    if b < 2:
                        sample_sig(b)
                    if 1 <= b < 3:
                        sample_turned(b - 1)
                    plain(gv, b % 2, b, None)
                    step(n, True)
                act.wait_ge(o_full, c.take(o_full))
                A(yc[0][:, :, SEQ:T], bo[:, 0:P].rearrange("p (a n) -> p a n", a=CT), ACT.Copy)
                act.wait_ge(yc_full, c.seen(yc_full))
                c.skip(yc_full)
                A(otmp[:, :], bo[:, 0:P], ACT.Copy).then_inc(o_hi, c.up(o_hi))
                act.wait_ge(acc_free[3], c.seen(acc_free[3]))
                A(gv[:, 0:2, :], gv[:, 0:2, :], ACT.Gelu).then_inc(gelu_v, c.up(gelu_v))
                for n in range(1, 4):
                    hi(used=acc_full[3])
                    for b in range(4):
                        plain(gv if n == 1 else gu, 2 * (n % 2) + b % 2, b, None, ACT.Gelu)
                act.wait_ge(tok_var, c.take(tok_var))
                A(rs[:, 0, :], mv[:, :, 1:2].rearrange("p a o -> p (a o)"), ACT.Sqrt, bias=eps[:, 0:1]).then_inc(
                    tok_std, c.up(tok_std))

                def gates(i, n, after=None):
                    hi(CHUNK // 2, used=acc_full[3])
                    act.wait_ge(m_sum, c.seen(m_sum))
                    for b in range(4):
                        act.wait_ge(acc_full[b], c.take(acc_full[b]))
                        act.sem_inc(passed, 1)
                        A(tmp[:, b, :], ps[b][:, 0:HALF], ACT.Sigmoid,
                                   bias=col(par, PAR["b_gate"] + 8 * BRANCHES[n] + 2 * i + b % 2)).then_inc(
                                       acc_free[b], c.up(acc_free[b]))
                        if after:
                            after(b)

                def products(i, n):
                    hi(used=acc_full[3], parts=2)
                    for b in range(4):
                        c.skip(acc_full[b])
                        c.skip(acc_free[b])
                        if n == 1:
                            c.skip(m_sum)
                        if n == 2:
                            act.wait_ge(m_sum, c.take(m_sum))
                            A(row(mh, 2 * i + b % 2, *((b // 2) * HALF, (b // 2 + 1) * HALF)),
                                       row(merged, 2 * i + b % 2, *((b // 2) * HALF, (b // 2 + 1) * HALF)),
                                       ACT.Copy).then_inc(m_hi, c.up(m_hi))

                def conv_write(h):
                    ln_root()
                    for t in range(CT):
                        if t % 2 == 0:
                            act.wait_ge(ln_norm, c.take(ln_norm))
                        A(acc[:, t, dcol(h)], sqc[:, t, :], ACT.Silu, scale=col(par, PAR["conv_g"] + t),
                          bias=col(par, PAR["conv_bb"] + t))
                        A(ya[0][:, t, dcol(h)], sqc[:, t, :], ACT.Silu, scale=col(par, PAR["conv_g"] + t),
                          bias=col(par, PAR["conv_bb"] + t)).then_inc(ln_hi, c.up(ln_hi))

                for n in range(3):
                    if n == 0:
                        def mixed_hi(b):
                            for g_ in range(CT if b == 2 else 0):
                                act.wait_ge(yb_sum, c.take(yb_sum))
                                A(yb[0][:, g_, :], gv[:, g_, :], ACT.Copy).then_inc(yb_hi, c.up(yb_hi))

                        gates(0, n, mixed_hi)
                        products(0, n)
                    elif n == 2:
                        gates(0, n, lambda b: conv_write(1) if b == 1 else None)
                        products(0, n)
                    else:
                        gates(0, n)
                        products(0, n)
                    passes = 2 if n == 1 else 3
                    with act.Fori(0, passes) as i, c.loop(f"branch{n}", passes, i):
                        gates(i + 1, n)
                        products(i + 1, n)
                    if n == 1:
                        act.wait_ge(glu_stored, c.take(glu_stored, 16 * 2 * CT))
                        act.wait_ge(sgu_stored, c.take(sgu_stored, 16))
                        gates(3, n, lambda b: ln_squares(CT, acc_view(acc, 0), sqc) if b == 0 else conv_write(0) if b == 2 else None)
                        products(3, n)
                        ln_squares(CT, acc_view(acc, 1), sqc)

                def skip(bs_):
                    for b in bs_:
                        c.skip(acc_full[b])
                        c.skip(acc_free[b])

                with act.Fori(0, 2) as r, c.loop("out0", 2, r):
                    hi(used=acc_full[3], parts=2)
                    skip((0, 1))
                    hi(used=acc_full[1], parts=2)
                    skip((2, 3))
                hi(used=acc_full[3], parts=2)
                skip((0, 1))
                ln_squares(KT, xT[:, :, dcol(0)], sq)
                hi(used=acc_full[1], parts=2)
                skip((2, 3))
                hi(used=acc_full[3], parts=2)
                ln_root()
                ln_write(KT, sq, xh, "ln1_g", "ln1_b", ACT.Identity, 0)
                skip((0, 1))
                hi(used=acc_full[1], parts=2)
                skip((2, 3))

                def gate_rows(b):
                    m = b % 2
                    act.wait_ge(acc_full[b], c.take(acc_full[b]))
                    if b < 2:
                        A(gex[:, m, 2:2 + HALF], ps[b][:, 0:HALF], ACT.Copy).then_inc(acc_free[b], c.up(acc_free[b]))
                    else:
                        A(gex[:, m, 2 + HALF:2 + SEQ], ps[b][:, 0:BP], ACT.Copy)
                        A(gex[:, m, 4 + SEQ:GEX], ps[b][:, BP:HALF], ACT.Copy).then_inc(acc_free[b], c.up(acc_free[b]))

                def conv_open(i):
                    act.wait_ge(acc_free[3], c.seen(acc_free[3]))
                    act.wait_ge(gex_full, c.take(gex_full, 2))
                    for m in range(2):
                        t = 2 * i + m
                        A(cbuf[:, m, :], gex[:, m, 0:GEX - 2], ACT.Identity, scale=col(par, PAR["fw"] + t),
                                   bias=col(par, PAR["fb"] + t)).then_inc(tap0_full, c.up(tap0_full))
                    for m in range(2):
                        act.wait_ge(conv3_full, c.take(conv3_full))
                        A(cbuf[:, m, :], cbuf[:, m, :], ACT.Gelu).then_inc(fgelu_full, c.up(fgelu_full))

                def f_rows(i, b):
                    c.skip(acc_full[b])
                    act.wait_ge(acc_free[b], c.take(acc_free[b]))
                    A(row(fhh[b // 2], 2 * i + b % 2, 0, HALF), tmp[:, b, :], ACT.Copy).then_inc(f_hi, c.up(f_hi))

                hi(used=acc_full[3])
                gate_rows(0)
                gate_rows(1)
                ln_squares(KT, xT[:, :, dcol(1)], sq)
                ln_root()
                ln_write(KT, sq, xh, "ln1_g", "ln1_b", ACT.Identity, 1)
                gate_rows(2)
                gate_rows(3)
                hi(used=acc_full[3])
                conv_open(0)
                for b in range(4):
                    f_rows(0, b)
                with act.Fori(0, 10) as i, c.loop("up", 10, i):
                    hi(used=acc_full[3])
                    for b in range(4):
                        gate_rows(b)
                    hi(used=acc_full[3])
                    conv_open(i + 1)
                    for b in range(4):
                        f_rows(i + 1, b)

                def down(i, middle=()):
                    for j in range(len(KGROUPS)):
                        nxt = KGROUPS[(j + 1) % len(KGROUPS)] * 512
                        hi(nxt, acc_full[3] if j == 0 else part_used[(j - 1) % 2], 2 if j < len(KGROUPS) - 1 else 1)
                        if j < len(KGROUPS) - 1:
                            c.skip(part_used[j % 2])
                        if 1 <= j <= len(middle):
                            middle[j - 1]()
                    skip(range(4))

                with act.Fori(0, 2) as r, c.loop("down0", 2, r):
                    down(0)
                down(0, (lambda: ln_squares(KT, xT[:, :, dcol(0)], sq), ln_root,
                         lambda: ln_write(KT, sq, xh, "ln2_g", "ln2_b", ACT.Identity, 0)))
                down(1)
                hi(used=acc_full[3])
                ln_squares(KT, xT[:, :, dcol(1)], sq)
                ln_root()
                ln_write(KT, sq, xh, "ln2_g", "ln2_b", ACT.Identity, 1)

        @block.vector
        def _(dve):
            c = Count("dve", adds)
            v = nc.vector

            dve.wait_ge(consts, 19)
            for h in range(2):
                for t in range(KT):
                    dve.wait_ge(x_hi, c.take(x_hi))
                    v.tensor_tensor(xl[:, t, dcol(h)], xT[:, t, dcol(h)], xh[:, t, dcol(h)].bitcast(F32),
                                             ALU.subtract).then_inc(x_ready[h], c.up(x_ready[h]))

            def rest_lo(s, size=CHUNK):
                n = size // 2
                dve.wait_ge(hi_rest[s], c.take(hi_rest[s]))
                v.tensor_tensor(wl[s][:, n:size], raw[s][:, n:size], wh[s][:, n:size].bitcast(F32),
                                ALU.subtract).then_inc(rest_full[s], c.up(rest_full[s]))

            def ln_open(nt, src):
                dve.wait_ge(vec, c.seen(vec))
                v.tensor_reduce(st0[:, :], src.rearrange("p k t -> p t k"), AX_X, ALU.add).then_inc(
                    ln_sum, c.up(ln_sum))

            def ln_centre(nt, src):
                dve.wait_ge(ln_mean, c.take(ln_mean))
                n = nt // 2
                for j in range(2):
                    mean = bo[:, 0:HALF].unsqueeze(1).broadcast_to([P, n, HALF])
                    part = src[:, j * n:(j + 1) * n]
                    v.tensor_tensor(part, part, mean, ALU.subtract).then_inc(ln_cent, c.up(ln_cent))

            def ln_squares(nt, buf):
                dve.wait_ge(ln_sq, c.take(ln_sq, 2))
                v.tensor_reduce(st0[:, :], buf[:, 0:nt, :].rearrange("p k t -> p t k"), AX_X, ALU.add).then_inc(
                    ln_ssum, c.up(ln_ssum))

            def ln_norm_(nt, src, buf):
                dve.wait_ge(ln_std, c.take(ln_std))
                v.reciprocal(st2[:, :], st1[:, :]).then_inc(vec, c.up(vec))
                dve.wait_ge(vec, c.seen(vec))
                n = nt // 2
                for j in range(2):
                    r = st2[:, :].unsqueeze(1).broadcast_to([P, n, HALF])
                    v.tensor_tensor(buf[:, j * n:(j + 1) * n, :], src[:, j * n:(j + 1) * n], r, ALU.mult).then_inc(
                        ln_norm, c.up(ln_norm))

            def ln_value(gname, bname, h):
                dve.wait_ge(ln_norm, c.seen(ln_norm))
                for t in range(KT):
                    v.tensor_scalar(xT[:, t, dcol(h)], sq[:, t, :], col(par, PAR[gname] + t),
                                        col(par, PAR[bname] + t), ALU.mult, ALU.add).then_inc(vec, c.up(vec))

            def ln_finish(src, gname, bname, h):
                dve.wait_ge(ln_std, c.take(ln_std))
                v.reciprocal(st2[:, :], st1[:, :]).then_inc(vec, c.up(vec))
                dve.wait_ge(vec, c.seen(vec))
                n = KT // 2
                for j in range(2):
                    r = st2[:, :].unsqueeze(1).broadcast_to([P, n, HALF])
                    v.tensor_tensor(sq[:, j * n:(j + 1) * n, :], src[:, j * n:(j + 1) * n], r, ALU.mult).then_inc(
                        ln_norm, c.up(ln_norm))
                    dve.wait_ge(ln_norm, c.seen(ln_norm))
                    for t in range(j * n, (j + 1) * n + 1):
                        if t < (j + 1) * n:
                            v.tensor_scalar(xT[:, t, dcol(h)], sq[:, t, :], col(par, PAR[gname] + t),
                                            col(par, PAR[bname] + t), ALU.mult, ALU.add).then_inc(vec, c.up(vec))
                        if t > j * n:
                            dve.wait_ge(vec, c.seen(vec, 1 if t < (j + 1) * n else 0))
                            dve.wait_ge(ln_hi, c.take(ln_hi))
                            v.tensor_tensor(xl[:, t - 1, dcol(h)], xT[:, t - 1, dcol(h)],
                                            xh[:, t - 1, dcol(h)].bitcast(F32),
                                            ALU.subtract).then_inc(x_ready[h], c.up(x_ready[h]))

            def ln_lo(h):
                dve.wait_ge(vec, c.seen(vec))
                for t in range(KT):
                    dve.wait_ge(ln_hi, c.take(ln_hi))
                    v.tensor_tensor(xl[:, t, dcol(h)], xT[:, t, dcol(h)], xh[:, t, dcol(h)].bitcast(F32),
                                             ALU.subtract).then_inc(x_ready[h], c.up(x_ready[h]))

            def skip(bs_):
                for b in bs_:
                    c.skip(acc_full[b])
                    c.skip(acc_free[b])

            def attend(b, n, m1, m0, w):
                dve.wait_ge(sig_full[b], c.take(sig_full[b]))
                weights(b, n, m1, m0, w, b)

            def weights(b, n, m1, m0, w, done):
                v.tensor_tensor(keep[b][:, n - w:n], keep[b][:, n - w:n], m1[:, 0:w], ALU.max).then_inc(vec, c.up(vec))
                v.tensor_tensor(beta[b][:, n - w:n], beta[b][:, n - w:n], m0[:, 0:w], ALU.mult).then_inc(vec, c.up(vec))
                v.memset(keep[b][:, n:n + 1], 1.0).then_inc(vec, c.up(vec))
                dve.wait_ge(vec, c.seen(vec))
                back = slice(n - 1, None, -1)
                v.tensor_tensor_scan(keep[b][:, 0:n][:, ::-1], keep[b][:, 0:n][:, ::-1],
                                         zero[:, 0:1].broadcast_to([P, n]), 1.0, ALU.mult, ALU.add).then_inc(
                                             vec, c.up(vec))
                dve.wait_ge(vec, c.seen(vec))
                v.tensor_tensor(beta[b][:, 0:n], beta[b][:, 0:n], keep[b][:, 1:n + 1], ALU.mult).then_inc(
                    at_full[done], c.up(at_full[done]))

            def rows_lo(u):
                dve.wait_ge(o_hi, c.take(o_hi))
                ht, i = u // 4, u % 4
                cols = slice(i * P, (i + 1) * P)
                v.tensor_tensor(yc[1][:, ht, cols], otmp[:, :], yc[0][:, ht, cols].bitcast(F32), ALU.subtract).then_inc(
                    yc_full, c.up(yc_full))

            def step(n, end):
                if not end:
                    if n < STEPS:
                        attend(0, (n % 4 + 1) * P, past1, past0, P)
                else:
                    if n < STEPS:
                        attend(1, (n % 4 + 1) * P, past1, past0, P)
                    if 2 <= n <= STEPS + 1:
                        rows_lo(n - 2)

            def tap(j):
                for m in range(CT):
                    dve.wait_ge(vec, c.seen(vec, CT - 1))
                    v.scalar_tensor_tensor(out=acc[:, m, :], in0=glu_at(m, j), scalar=col(par, PAR["conv_w"] + j * CT + m),
                                               in1=acc[:, m, :], op0=ALU.mult, op1=ALU.add).then_inc(vec, c.up(vec))

            def glu_at(m, j):
                if isinstance(j, int):
                    return glu[:, m, j:j + CV]
                return glu[:, m, bass.ds(j, CV)]

            v.memset(st0[:, :], 0.0).then_inc(ln_sum, c.up(ln_sum))
            dve.wait_ge(ln_sum, c.seen(ln_sum))
            v.memset(st1[:, 0:1], 0.0).then_inc(ln_ssum, c.up(ln_ssum))
            c.skip(ln_mean)

            with dve.Fori(0, DEPTH) as r, c.loop("layer", DEPTH, r):
                dve.wait_ge(vec, c.seen(vec))
                v.memset(glu[:, :, 0:HIST], 0.0).then_inc(vec, c.up(vec))
                for n in range(6):
                    skip(range(4))
                for t in range(5):
                    dve.wait_ge(v_turned, c.take(v_turned))
                    n = P if t < 4 else DEC
                    v.tensor_copy(vtok[0:n, t, :], bt[0:n, :]).then_inc(vtok_full, c.up(vtok_full))
                dve.wait_ge(small_full, c.take(small_full, 160))
                for n in range(4):
                    for b in range(4):
                        step(4 * n + b, False)
                        if n % 2 == 0:
                            skip((b,))
                        else:
                            m = n // 2 * 2 + b % 2
                            dve.wait_ge(acc_free[b], c.seen(acc_free[b]))
                            dve.wait_ge(acc_full[b], c.take(acc_full[b]))
                            o = HIST + (b // 2) * HALF
                            if b < 2:
                                v.tensor_tensor(glu[:, m, o:o + HALF], ps[b][:, 0:HALF], tmp[:, b, :],
                                                         ALU.mult).then_inc(acc_free[b], c.up(acc_free[b]))
                            else:
                                v.tensor_tensor(glu[:, m, o:o + BP], ps[b][:, 0:BP], tmp[:, b, 0:BP], ALU.mult).then_inc(
                                    vec, c.up(vec))
                                v.tensor_tensor(glu[:, m, GT - DEC:GT], ps[b][:, BP:HALF], tmp[:, b, BP:HALF],
                                                         ALU.mult).then_inc(acc_free[b], c.up(acc_free[b]))
                        step(4 * n + b, True)
                for b in range(4):
                    n = STEPS + b
                    step(n, False)
                    if b < 2:
                        dve.wait_ge(sig_full[0], c.take(sig_full[0]))
                        dve.wait_ge(sig_full[1], c.take(sig_full[1]))
                        weights(b, PAST + DEC, spast1, spast0, DEC, b)
                    skip((b,))
                    step(n, True)
                dve.wait_ge(o_hi, c.take(o_hi))
                v.tensor_tensor(yc[1][:, :, SEQ:T], otmp[:, :].rearrange("p (a n) -> p a n", a=CT),
                                         yc[0][:, :, SEQ:T].bitcast(F32), ALU.subtract).then_inc(yc_full, c.up(yc_full))
                dve.wait_ge(at_full[1], c.seen(at_full[1]))
                dve.wait_ge(acc_free[3], c.seen(acc_free[3]))
                dve.wait_ge(vec, c.seen(vec))
                for m in range(CT):
                    v.tensor_scalar(acc[:, m, :], glu_at(m, 0), col(par, PAR["conv_w"] + m),
                                             col(par, PAR["conv_b"] + m), ALU.mult, ALU.add).then_inc(
                                                 glu_full, c.up(glu_full))
                dve.wait_ge(glu_full, c.seen(glu_full))
                at = 1
                for n in range(4):
                    if n > 0:
                        skip(range(4))
                    for _ in range(UV_TAPS[n]):
                        tap(at)
                        at += 1
                    if n == 2:
                        for t in range(5):
                            dve.wait_ge(tok_turned, c.take(tok_turned))
                            r = P if t < 4 else DEC
                            v.tensor_copy(ntok[0:r, t, :], bt[0:r, :]).then_inc(tok_full, c.up(tok_full))
                            dve.wait_ge(tok_full, c.seen(tok_full))
                            v.bn_stats(bnst[0:r, t, :], ntok[0:r, t, :]).then_inc(vec, c.up(vec))
                            dve.wait_ge(vec, c.seen(vec))
                            dve.sem_inc(passed, 1)
                            v.bn_aggr(mv[0:r, t, :], bnst[0:r, t, :]).then_inc(vec, c.up(vec))
                dve.wait_ge(vec, c.seen(vec))
                v.memset(rs[:, 1, :], 0.0).then_inc(tok_var, c.up(tok_var))
                dve.wait_ge(tok_std, c.take(tok_std))
                v.reciprocal(rs[:, 1, :], rs[:, 0, :]).then_inc(vec, c.up(vec))
                dve.wait_ge(vec, c.seen(vec))
                for t in (4, 0, 1, 2, 3):
                    r = P if t < 4 else DEC
                    v.tensor_scalar(ntok[0:r, t, :], ntok[0:r, t, :], mv[0:r, t, 0:1], rs[0:r, 1, t:t + 1],
                                        ALU.subtract, ALU.mult).then_inc(vec, c.up(vec))
                dve.wait_ge(vec, c.seen(vec))
                for t in (4, 0, 1, 2, 3):
                    r = P if t < 4 else DEC
                    v.tensor_tensor(ntok[0:r, t, :], ntok[0:r, t, :], bc[0:r, 0, :], ALU.mult).then_inc(vec, c.up(vec))
                dve.wait_ge(vec, c.seen(vec))
                for t in (0, 1, 2, 3, 4):
                    r = P if t < 4 else DEC
                    ins = v.tensor_tensor(ntok[0:r, t, :], ntok[0:r, t, :], bc[0:r, 1, :], ALU.add)
                    if t < 4:
                        ins.then_inc(vec, c.up(vec))
                    else:
                        ins.then_inc(ntok_full, c.up(ntok_full))
                for g_ in range(CT):
                    dve.wait_ge(mixed, c.take(mixed, 2 if g_ == 0 else 1))
                    bias = bc[:, 2, g_ * P:(g_ + 1) * P]
                    v.tensor_tensor(gv[:, g_, 0:SEQ].rearrange("p (a n) -> p a n", a=4),
                                        bs[g_ % 2][:, :].rearrange("p (a n) -> p a n", a=4),
                                        bias.unsqueeze(1).broadcast_to([P, 4, P]), ALU.add).then_inc(vec, c.up(vec))
                    v.tensor_tensor(gv[:, g_, SEQ:T], bt[:, g_ * DEC:(g_ + 1) * DEC],
                                             bias[:, 0:DEC], ALU.add).then_inc(mixed_used, c.up(mixed_used))
                    dve.wait_ge(mixed_used, c.seen(mixed_used))
                    dve.wait_ge(vec, c.seen(vec))
                    v.tensor_tensor(gv[:, g_, :], gv[:, g_, :], gu[:, g_, :], ALU.mult).then_inc(yb_sum, c.up(yb_sum))
                    dve.wait_ge(yb_sum, c.seen(yb_sum))
                for g_ in range(CT):
                    dve.wait_ge(yb_hi, c.take(yb_hi))
                    v.tensor_tensor(yb[1][:, g_, :], gv[:, g_, :], yb[0][:, g_, :].bitcast(F32),
                                             ALU.subtract).then_inc(yb_full, c.up(yb_full))

                def products(i, n):
                    for b in range(4):
                        skip((b,))
                    rest_lo(0)

                    def low(b):
                        t, cols = 2 * i + b % 2, (b // 2 * HALF, (b // 2 + 1) * HALF)
                        dve.wait_ge(m_hi, c.take(m_hi))
                        v.tensor_tensor(row(ml, t, *cols), row(merged, t, *cols), row(mh, t, *cols).bitcast(F32),
                                        ALU.subtract).then_inc(m_ready[b // 2], c.up(m_ready[b // 2]))

                    for b in range(4):
                        t, cols = 2 * i + b % 2, (b // 2 * HALF, (b // 2 + 1) * HALF)
                        dve.wait_ge(acc_free[b], c.seen(acc_free[b]))
                        dve.wait_ge(acc_full[b], c.take(acc_full[b]))
                        if n == 0:
                            v.tensor_tensor(row(merged, t, *cols), ps[b][:, 0:HALF], tmp[:, b, :], ALU.mult).then_inc(
                                acc_free[b], c.up(acc_free[b]))
                        else:
                            v.tensor_tensor(tmp[:, b, :], ps[b][:, 0:HALF], tmp[:, b, :], ALU.mult).then_inc(
                                acc_free[b], c.up(acc_free[b]))
                            dve.wait_ge(acc_free[b], c.seen(acc_free[b]))
                            done = v.tensor_tensor(row(merged, t, *cols), row(merged, t, *cols), tmp[:, b, :], ALU.add)
                            done.then_inc(m_sum, c.up(m_sum))
                        if n == 2 and b == 2:
                            low(0)
                            low(1)
                    if n == 2:
                        low(2)
                        low(3)

                products(0, 0)
                with dve.Fori(0, 3) as i, c.loop("branch0", 3, i):
                    for j in range(B_TAPS):
                        tap(i * B_TAPS + (at + j))
                    products(i + 1, 0)
                at += 3 * B_TAPS
                for j in range(C_FIRST):
                    tap(at + j)
                at += C_FIRST
                products(0, 1)
                with dve.Fori(0, 2) as i, c.loop("branch1", 2, i):
                    for j in range(C_TAPS):
                        tap(i * C_TAPS + (at + j))
                    products(i + 1, 1)
                dve.wait_ge(vec, c.seen(vec))
                v.tensor_copy(st2[:, 0:P].rearrange("p (a n) -> p a n", a=CT), acc[:, :, SCOL:SCOL + DEC]).then_inc(
                    vec, c.up(vec))
                dve.wait_ge(vec, c.seen(vec))
                v.tensor_copy(acc[:, :, SEQ:T], st2[:, 0:P].rearrange("p (a n) -> p a n", a=CT)).then_inc(
                    vec, c.up(vec))

                def conv_lo(h):
                    ln_norm_(CT, acc_view(acc, h), sqc)
                    for t in range(CT):
                        dve.wait_ge(ln_hi, c.take(ln_hi))
                        v.tensor_tensor(ya[1][:, t, dcol(h)], acc[:, t, dcol(h)],
                                        ya[0][:, t, dcol(h)].bitcast(F32), ALU.subtract).then_inc(
                                            ya_full, c.up(ya_full))

                ln_open(CT, acc_view(acc, 0))
                ln_centre(CT, acc_view(acc, 0))
                ln_squares(CT, sqc)
                conv_lo(0)
                ln_open(CT, acc_view(acc, 1))
                products(3, 1)
                ln_centre(CT, acc_view(acc, 1))
                ln_squares(CT, sqc)
                conv_lo(1)
                products(0, 2)
                with dve.Fori(0, 3) as i, c.loop("branch2", 3, i):
                    products(i + 1, 2)

                def residual(t, b, h):
                    cols = (h * HALF, (h + 1) * HALF)
                    dve.wait_ge(acc_full[b], c.take(acc_full[b]))
                    v.scalar_tensor_tensor(out=row(xT, t, *cols), in0=row(xT, t, *cols), scalar=ALPHA,
                                                    in1=ps[b][:, 0:HALF], op0=ALU.mult, op1=ALU.add).then_inc(
                                                        acc_free[b], c.up(acc_free[b]))

                x0, x1 = xT[:, :, dcol(0)], xT[:, :, dcol(1)]
                with dve.Fori(0, 2) as i, c.loop("out0", 2, i):
                    for b in range(4):
                        if b % 2 == 0:
                            rest_lo(1 - b // 2)
                        residual(4 * i + b, b, 0)
                dve.wait_ge(acc_free[3], c.seen(acc_free[3]))
                rest_lo(1)
                ln_open(KT, x0)
                residual(0, 0, 1)
                residual(1, 1, 1)
                ln_centre(KT, x0)
                rest_lo(0)
                ln_squares(KT, sq)
                residual(2, 2, 1)
                residual(3, 3, 1)
                rest_lo(1)
                ln_norm_(KT, x0, sq)
                ln_value("ln1_g", "ln1_b", 0)
                residual(4, 0, 1)
                residual(5, 1, 1)
                ln_lo(0)
                rest_lo(0)
                residual(6, 2, 1)
                residual(7, 3, 1)
                dve.wait_ge(acc_free[3], c.seen(acc_free[3]))
                ln_open(KT, x1)
                ln_centre(KT, x1)
                ln_squares(KT, sq)
                ln_finish(x1, "ln1_g", "ln1_b", 1)

                def conv_close(i):
                    skip(range(4))
                    for m in range(2):
                        t = 2 * i + m
                        dve.wait_ge(tap0_full, c.take(tap0_full))
                        v.scalar_tensor_tensor(out=cbuf[:, m, :], in0=gex[:, m, 1:GEX - 1],
                                                   scalar=col(par, PAR["fw"] + FT + t), in1=cbuf[:, m, :],
                                                   op0=ALU.mult, op1=ALU.add).then_inc(vec, c.up(vec))
                        v.tensor_copy(row(fst, t, 0, 2), gex[:, m, SEQ:SEQ + 2]).then_inc(vec, c.up(vec))
                        v.tensor_copy(row(fst, t, 2, 4), gex[:, m, GEX - 2:GEX]).then_inc(vec, c.up(vec))
                        dve.wait_ge(vec, c.seen(vec))
                        v.scalar_tensor_tensor(out=cbuf[:, m, :], in0=gex[:, m, 2:GEX],
                                                        scalar=col(par, PAR["fw"] + 2 * FT + t), in1=cbuf[:, m, :],
                                                        op0=ALU.mult, op1=ALU.add).then_inc(
                                                            conv3_full, c.up(conv3_full))

                def history(i):
                    for m in range(2):
                        ins = v.tensor_copy(gex[:, m, 2 + SEQ:4 + SEQ], row(fhist, 2 * i + m, 0, 2))
                        ins.then_inc(gex_full, c.up(gex_full))

                def f_rows(i):
                    for b in range(4):
                        m, h = b % 2, b // 2
                        dve.wait_ge(acc_full[b], c.take(acc_full[b]))
                        if b < 2:
                            dve.wait_ge(fgelu_full, c.take(fgelu_full))
                            v.tensor_tensor(tmp[:, b, :], ps[b][:, 0:HALF], cbuf[:, m, 0:HALF], ALU.mult).then_inc(
                                acc_free[b], c.up(acc_free[b]))
                        else:
                            v.tensor_tensor(tmp[:, b, 0:BP], ps[b][:, 0:BP], cbuf[:, m, HALF:SEQ], ALU.mult).then_inc(
                                vec, c.up(vec))
                            v.tensor_tensor(tmp[:, b, BP:HALF], ps[b][:, BP:HALF], cbuf[:, m, SEQ + 2:GEX - 2],
                                                     ALU.mult).then_inc(acc_free[b], c.up(acc_free[b]))
                    for b in range(4):
                        dve.wait_ge(f_hi, c.take(f_hi))
                        v.tensor_tensor(row(fll[b // 2], 2 * i + b % 2, 0, HALF), tmp[:, b, :],
                                                 row(fhh[b // 2], 2 * i + b % 2, 0, HALF).bitcast(F32),
                                                 ALU.subtract).then_inc(f_ready, c.up(f_ready))

                history(0)
                conv_close(0)
                f_rows(0)
                with dve.Fori(0, 10) as i, c.loop("up", 10, i):
                    history(i + 1)
                    conv_close(i + 1)
                    f_rows(i + 1)

                def rests(js):
                    for j in js:
                        rest_lo(j % 2, KGROUPS[j] * 512)

                with dve.Fori(0, 2) as i, c.loop("down0", 2, i):
                    rests(range(1, 6))
                    for b in range(4):
                        residual(4 * i + b, b, 0)
                dve.wait_ge(acc_free[3], c.seen(acc_free[3]))
                ln_open(KT, x0)
                rests((1, 2))
                ln_centre(KT, x0)
                ln_squares(KT, sq)
                rests((3,))
                ln_norm_(KT, x0, sq)
                rests((4,))
                ln_value("ln2_g", "ln2_b", 0)
                ln_lo(0)
                rests((5,))
                for b in range(4):
                    residual(b, b, 1)
                rests(range(1, 6))
                for b in range(4):
                    residual(4 + b, b, 1)
                dve.wait_ge(acc_free[3], c.seen(acc_free[3]))
                ln_open(KT, x1)
                ln_centre(KT, x1)
                ln_squares(KT, sq)
                ln_finish(x1, "ln2_g", "ln2_b", 1)
                dve.wait_ge(ffn_stored, c.take(ffn_stored, 16))
                dve.wait_ge(x_ready[1], c.seen(x_ready[1]))
                v.memset(st0[:, 0:1], 0.0).then_inc(layer_done, c.up(layer_done))

        @block.tensor
        def _(pe):
            c = Count("pe", adds)
            mm = pe.matmul
            turn = [0]
            turned_by = [None]
            small_by = [None]
            pe.wait_ge(consts, 19)

            def arrived(parts=1):
                s = turn[0] % 2
                turn[0] += 1
                pe.wait_ge(lo_full[s], c.take(lo_full[s]))
                if parts == 2:
                    pe.wait_ge(rest_full[s], c.take(rest_full[s]))
                return s

            def three(out, s, at, xs, start, stop):
                a, b = wh[s][:, at:at + P], wl[s][:, at:at + P]
                mm(out, a, xs[0], start=start, stop=False)
                mm(out, a, xs[1], start=False, stop=False)
                return mm(out, b, xs[0], start=False, stop=stop)

            def unit(s, b, m, xs, nk, each=None, mid=None, h=None, spare=None):
                if spare is None:
                    pe.wait_ge(acc_free[b], c.prev(acc_free[b]))
                else:
                    c.skip(acc_free[b])
                for t in range(nk):
                    if each:
                        each(t)
                    last = three((spare or ps[b])[:, 0:HALF], s, t * 256 + m * P, [x[:, t, dcol(b // 2 if h is None else h)] for x in xs],
                                 t == 0, t == nk - 1)
                    if mid and t == nk // 2 - 1:
                        mid()
                last.then_inc(acc_full[b], c.up(acc_full[b]))

            def chunk(xs=(xh, xl), nk=KT, first=None, mid=None, end=None, parts=1):
                s = arrived(parts)
                for b in range(4):
                    unit(s, b, b % 2, xs, nk, first and (lambda t, b=b: first(t, b)), mid and (lambda b=b: mid(b)))
                    if end:
                        end(b)

            def half_chunk(h, banks, src, w=256):
                s = arrived(2)
                for m, b in enumerate(banks):
                    pe.wait_ge(acc_free[b], c.prev(acc_free[b]))
                    for t in range(KT):
                        last = three(ps[b][:, 0:HALF], s, t * w + m * P, [x[:, t, dcol(h)] for x in src],
                                     t == 0, t == KT - 1)
                    last.then_inc(acc_full[b], c.up(acc_full[b]))

            def ln_mean_(ones):
                pe.wait_ge(ln_sum, c.take(ln_sum))
                mm(bo[:, 0:HALF], ones[:, :], st0[:, :], start=True, stop=True).then_inc(ln_mean, c.up(ln_mean))

            def ln_var_(ones):
                pe.wait_ge(ln_ssum, c.take(ln_ssum))
                mm(bo[:, 0:HALF], ones[:, :], st0[:, :], start=True, stop=True).then_inc(ln_var, c.up(ln_var))

            def scores(u, b):
                ht, i = u // 4, u % 4
                rows = slice(DH * b, DH * b + DH)
                pe.wait_ge(sig_full[b], c.prev(sig_full[b]))
                mm(bs[b][:, 0:(i + 1) * P], q[rows, ht, i * P:(i + 1) * P], k[rows, ht, 0:(i + 1) * P],
                            start=True, stop=True).then_inc(s_full[b], c.up(s_full[b]))

            def turn_bank():
                if turned_by[0] is not None:
                    pe.wait_ge(turned_by[0], c.seen(turned_by[0]))

            def turns(u, b):
                pe.wait_ge(at_full[b], c.take(at_full[b]))
                turn_bank()
                for kb in range(u % 4 + 1):
                    last = pe.transpose(bt[:, kb * P:(kb + 1) * P], beta[b][:, kb * P:(kb + 1) * P], ident[:, :])
                last.then_inc(t_full, c.up(t_full))
                c.skip(att_full[b])
                turned_by[0] = att_full[b]

            def values(u, b):
                ht, i = u // 4, u % 4
                pe.wait_ge(att_full[b], c.seen(att_full[b]))
                if b == 0:
                    pe.wait_ge(o_hi, c.prev(o_hi))
                for kb in range(i + 1):
                    last = mm(bo[DH * b:DH * b + DH, 0:P], vtok[:, kb, (2 * ht + b) * DH:(2 * ht + b + 1) * DH],
                              att[b][:, kb * P:(kb + 1) * P], start=kb == 0, stop=kb == i)
                if b == 1:
                    last.then_inc(o_full, c.up(o_full))

            def step(n, end):
                if not end:
                    if 1 <= n <= STEPS:
                        turns(n - 1, 0)
                    if 2 <= n <= STEPS + 1:
                        values(n - 2, 1)
                    if n < STEPS:
                        scores(n, 0)
                else:
                    if 1 <= n <= STEPS:
                        values(n - 1, 0)
                        turns(n - 1, 1)
                    if n < STEPS:
                        scores(n, 1)

            def sample_scores(s):
                rows = slice(DH * s, DH * s + DH)
                for b, (keys, n) in enumerate(((kc[rows, :, :], PAST), (k[rows, :, SEQ:T], DEC))):
                    pe.wait_ge(sig_full[b], c.prev(sig_full[b]))
                    pe.sem_inc(passed, 1)
                    for ht in range(CT):
                        last = mm(bs[b][DEC * ht:DEC * ht + DEC, 0:n], q[rows, ht, SEQ:T], keys[:, ht, :],
                                  start=True, stop=True)
                    last.then_inc(s_full[b], c.up(s_full[b]))

            def sample_turns(s):
                pe.wait_ge(at_full[s], c.take(at_full[s]))
                turn_bank()
                for kb in range(4):
                    last = pe.transpose(bt[:, kb * P:(kb + 1) * P], beta[s][:, kb * P:(kb + 1) * P], ident[:, :])
                last.then_inc(t_full, c.up(t_full))
                c.skip(att_full[s])
                pe.wait_ge(att_full[s], c.seen(att_full[s]))
                pe.transpose(bt[0:DEC, 0:P], beta[s][:, PAST:PAST + DEC], ident[:, :]).then_inc(t_full, c.up(t_full))
                c.skip(att_full[s])
                turned_by[0] = att_full[s]

            def sample_values(s):
                pe.wait_ge(att_full[s], c.seen(att_full[s]))
                if s == 0:
                    pe.wait_ge(o_hi, c.prev(o_hi))
                for ht in range(CT):
                    h = 2 * ht + s
                    out = bo[DH * s:DH * s + DH, ht * DEC:(ht + 1) * DEC]
                    for kb in range(4):
                        mm(out, vc[:, kb, h * DH:(h + 1) * DH], att[s][:, kb * P + ht * DEC:kb * P + (ht + 1) * DEC],
                           start=kb == 0, stop=False)
                    last = mm(out, vtok[0:DEC, 4, h * DH:(h + 1) * DH],
                              att[s][0:DEC, PAST + ht * DEC:PAST + (ht + 1) * DEC], start=False, stop=True)
                if s == 1:
                    last.then_inc(o_full, c.up(o_full))

            def turn_tokens(src, t, sig_to, by):
                n = P if t < 4 else DEC
                turn_bank()
                for m in range(CT):
                    last = pe.transpose(bt[0:n, m * P:(m + 1) * P], src[:, m, t * P:t * P + n], ident[:, :])
                last.then_inc(sig_to, c.up(sig_to))
                c.skip(by)
                turned_by[0] = by

            with pe.Fori(0, DEPTH) as r, c.loop("layer", DEPTH, r):
                turned_by[0] = None

                xs = (xh, xl)
                s0 = arrived()
                unit(s0, 0, 0, xs, KT, lambda t: pe.wait_ge(x_ready[0], c.take(x_ready[0])), h=0)
                ln_mean_(mean_d)
                unit(s0, 1, 1, xs, KT, h=0)
                s1 = arrived()
                unit(s1, 2, 0, xs, KT, h=0)
                unit(s1, 3, 1, xs, KT, h=0)
                ln_var_(mean_d)
                unit(s0, 0, 0, xs, KT, lambda t: pe.wait_ge(x_ready[1], c.take(x_ready[1])), h=1,
                     spare=bs[0])
                unit(s0, 1, 1, xs, KT, h=1, spare=bs[1])
                unit(s1, 2, 0, xs, KT, h=1)
                unit(s1, 3, 1, xs, KT, h=1)

                def turn_v(n):
                    def after(b):
                        t = 4 * n + b
                        if t < 5:
                            if t == 0:
                                for bb in range(4):
                                    pe.wait_ge(acc_free[bb], c.seen(acc_free[bb], 1))
                            turn_tokens(vfm, t, v_turned, vtok_full)
                    return after

                chunk()
                chunk(end=turn_v(0))
                chunk(end=turn_v(1))
                chunk()
                pe.wait_ge(small_full, c.take(small_full, 160))
                for b in range(4):
                    pe.wait_ge(acc_free[b], c.seen(acc_free[b]))
                for n in range(4):
                    chunk(mid=lambda b, n=n: step(4 * n + b, False), end=lambda b, n=n: step(4 * n + b, True))

                def mid(b):
                    step(STEPS + b, False)
                    if b < 2:
                        sample_scores(b)
                    if 1 <= b < 3:
                        sample_turns(b - 1)

                def end(b):
                    step(STEPS + b, True)
                    if 2 <= b:
                        sample_values(b - 2)

                chunk(mid=mid, end=end)
                chunk()

                def turn_gv(n):
                    def after(b):
                        t = 4 * n + b
                        if t == 0:
                            pe.wait_ge(gelu_v, c.take(gelu_v))
                            for bb in range(4):
                                pe.wait_ge(acc_free[bb], c.seen(acc_free[bb], 1 if bb == 0 else 0))
                        if t < 5:
                            turn_tokens(gv, t, tok_turned, tok_full)
                    return after

                chunk(end=turn_gv(0))
                chunk(end=turn_gv(1))

                def mix():
                    pe.wait_ge(ntok_full, c.take(ntok_full))
                    pe.wait_ge(sgu_masked, c.take(sgu_masked))
                    turn_bank()
                    for g_ in range(CT):
                        if g_ > 1:
                            pe.wait_ge(mixed_used, c.seen(mixed_used, CT - g_ + 1))
                        if g_ == 0:
                            for gg in range(CT):
                                last = mm(bt[:, gg * DEC:(gg + 1) * DEC], ntok[0:DEC, 4, gg * P:(gg + 1) * P],
                                          wsgu[0:DEC, gg, 0:DEC], start=True, stop=True)
                            last.then_inc(mixed, c.up(mixed))
                            c.skip(mixed_used, CT)
                        for t in range(4):
                            last = mm(bs[g_ % 2][:, t * P:(t + 1) * P], ntok[:, t, g_ * P:(g_ + 1) * P], wsgu[:, g_, :],
                                      start=True, stop=True)
                        last.then_inc(mixed, c.up(mixed))
                    turned_by[0] = mixed_used

                ybs = dict(xs=yb, nk=CT)
                chunk(end=lambda b: mix() if b == 2 else None)
                c.skip(yb_full, CT)
                chunk(**ybs, first=lambda t, b: pe.wait_ge(yb_full, c.seen(yb_full, CT - 1 - t)) if b == 0 else None)
                with pe.Fori(0, 3) as r, c.loop("branch0", 3, r):
                    chunk(parts=2)
                    chunk(**ybs)
                c.skip(yc_full, STEPS + 1)
                chunk(parts=2)
                pe.wait_ge(yc_full, c.seen(yc_full))
                chunk(xs=yc, nk=CT)
                with pe.Fori(0, 2) as r, c.loop("branch1", 2, r):
                    chunk(parts=2)
                    chunk(xs=yc, nk=CT)
                chunk(parts=2, end=lambda b: ln_mean_(mean_c) if b == 0 else ln_var_(mean_c) if b == 2 else None)
                chunk(xs=yc, nk=CT)
                ln_mean_(mean_c)
                chunk(parts=2, end=lambda b: ln_var_(mean_c) if b == 1 else None)

                def ya_tiles(t, b):
                    if b in (0, 2):
                        pe.wait_ge(ya_full, c.take(ya_full))
                chunk(xs=ya, nk=CT, first=ya_tiles)
                with pe.Fori(0, 3) as r, c.loop("branch2", 3, r):
                    chunk(parts=2)
                    chunk(xs=ya, nk=CT)

                pe.wait_ge(m_ready[0], c.take(m_ready[0], KT))
                pe.sem_inc(passed, 1)
                with pe.Fori(0, 2) as r, c.loop("out0", 2, r):
                    half_chunk(0, (0, 1), (mh, ml))
                    half_chunk(0, (2, 3), (mh, ml))
                pe.wait_ge(m_ready[1], c.take(m_ready[1], KT))
                for i in range(2):
                    half_chunk(1, (0, 1), (mh, ml))
                    if i == 0:
                        ln_mean_(mean_d)
                    half_chunk(1, (2, 3), (mh, ml))
                    if i == 0:
                        ln_var_(mean_d)

                s0 = arrived(2)
                unit(s0, 0, 0, (xh, xl), KT, lambda t: pe.wait_ge(x_ready[0], c.take(x_ready[0])))
                unit(s0, 1, 1, (xh, xl), KT)
                ln_mean_(mean_d)
                s1 = arrived()
                unit(s1, 0, 0, (xh, xl), KT)
                unit(s1, 1, 1, (xh, xl), KT)
                ln_var_(mean_d)
                unit(s0, 2, 0, (xh, xl), KT, lambda t: pe.wait_ge(x_ready[1], c.take(x_ready[1])))
                unit(s0, 3, 1, (xh, xl), KT)
                unit(s1, 2, 0, (xh, xl), KT)
                unit(s1, 3, 1, (xh, xl), KT)
                with pe.Fori(0, 10) as r, c.loop("up", 10, r):
                    chunk()
                    chunk()

                def down(h, middle=None):
                    at = 0
                    for j, kn in enumerate(KGROUPS):
                        s = arrived(2 if j else 1)
                        if h == 0 and j == len(KGROUPS) - 1:
                            pe.wait_ge(f_ready, c.seen(f_ready))
                        for b in range(4):
                            if j == 0:
                                pe.wait_ge(acc_free[b], c.prev(acc_free[b]))
                            for t in range(kn):
                                last = three(ps[b][:, 0:HALF], s, t * 512 + b * P,
                                             [f[h][:, at + t, :] for f in (fhh, fll)],
                                             j == 0 and t == 0, j == len(KGROUPS) - 1 and t == kn - 1)
                            if j == len(KGROUPS) - 1:
                                last.then_inc(acc_full[b], c.up(acc_full[b]))
                        if j < len(KGROUPS) - 1:
                            last.then_inc(part_used[s], c.up(part_used[s]))
                        at += kn
                        if middle and j in (0, 2):
                            middle[j // 2]()

                c.skip(f_ready, 4 * 11)
                pe.wait_ge(f_ready, c.seen(f_ready, 4))
                pe.sem_inc(passed, 1)
                with pe.Fori(0, 2) as r, c.loop("down0", 2, r):
                    down(0)
                down(1, (lambda: ln_mean_(mean_d), lambda: ln_var_(mean_d)))
                down(1)
            ln_mean_(mean_d)
            ln_var_(mean_d)


def acc_view(acc, h):
    return acc[:, :, h * HALF:(h + 1) * HALF]


def kernel(**inputs):
    import numpy as np
    import concourse.bacc as bacc
    from concourse.bass_utils import run_bass_kernel_spmd

    a = {n: np.asarray(v) for n, v in inputs.items()}

    def cols(w, n):
        L, K, C = w.shape
        return w.reshape(L, K // P, P, C // n, n).transpose(0, 3, 2, 1, 4).reshape(L, C // n, P, (K // P) * n)

    def chan(v, n):
        return v.reshape(DEPTH, -1, n, P).transpose(0, 3, 1, 2).reshape(DEPTH, P, -1)

    def feat(v):
        L, r, ch = v.shape
        return v.reshape(L, r, ch // P, P).transpose(0, 3, 2, 1)

    arrays = {
        "x_in": feat(np.concatenate([a["x_prompt"], a["x_sample"]], axis=1))[0],
        "win": cols(a["w_in"], 256).reshape(-1, P, CHUNK),
        "wbr": cols(a["w_branch"].reshape(DEPTH * 3, CH, D), 256).reshape(-1, P, CHUNK // 2),
        "wout": cols(a["w_out"], 256).reshape(-1, P, CHUNK),
        "wup": cols(a["w_up"], 256).reshape(-1, P, CHUNK),
        "wdn": cols(a["w_down"], 512).reshape(-1, P, FT * 512),
        "par_in": np.concatenate([chan(a["b_gate"], KT), chan(a["conv_w"], CT), chan(a["conv_b"], CT),
                                  chan(a["conv_ln_g"], CT), chan(a["conv_ln_b"], CT), chan(a["ln1_g"], KT),
                                  chan(a["ln1_b"], KT), chan(a["ln2_g"], KT), chan(a["ln2_b"], KT),
                                  chan(a["ffn_conv_w"], FT), chan(a["ffn_conv_b"], FT)], axis=2),
        "bc_in": np.broadcast_to(np.stack([a["sgu_ln_g"], a["sgu_ln_b"], a["sgu_b"].reshape(DEPTH, CH)], axis=1)
                                 .reshape(DEPTH, 1, 3 * CH), (DEPTH, P, 3 * CH)),
        "sguw_in": a["sgu_w"].transpose(0, 3, 1, 2).reshape(DEPTH, P, CH),
        "kc_in": feat(a["cache_sb_k"].reshape(DEPTH, PAST, CH)).reshape(DEPTH, P, CT * PAST),
        "vc_in": a["cache_sb_v"].reshape(DEPTH, 4, P, CH).transpose(0, 2, 1, 3).reshape(DEPTH, P, 4 * CH),
        "gh_in": a["state_conv_glu"].reshape(DEPTH, HIST, CT, P).transpose(0, 2, 3, 1).reshape(DEPTH * CT, P, HIST),
        "fh_in": feat(a["state_ffn_conv"].reshape(DEPTH, 2, FF)).reshape(DEPTH, P, FT * 2),
    }
    arrays = {n: np.ascontiguousarray(v) for n, v in arrays.items()}
    outs = {"y_out": (P, KT, T), "k_out": (DEPTH, P, CT * T), "v_out": (DEPTH, P, CT * T),
            "glu_out": (DEPTH * CT * 2, P, HIST), "ffn_out": (DEPTH, P, FT * 4), "sgu_out": (DEPTH, DEC, CH)}

    adds = {}
    for _ in range(2):
        nc = bacc.Bacc("TRN2", target_bir_lowering=False, num_devices=1, dynamic_dma_scratch_size=1024)
        ins = [nc.dram_tensor(n, v.shape, F32, kind="ExternalInput").ap() for n, v in arrays.items()]
        out = [nc.dram_tensor(n, s, F32, kind="ExternalOutput").ap() for n, s in outs.items()]
        trunk(nc, adds, *ins, *out)
    r = run_bass_kernel_spmd(nc, [arrays], core_ids=[0]).results[0]

    def rows(v):
        v = np.moveaxis(v, -1, -3)
        v = np.swapaxes(v, -1, -2)
        return v.reshape(*v.shape[:-2], -1)

    y = rows(r["y_out"])
    kk = rows(r["k_out"].reshape(DEPTH, P, CT, T)).reshape(DEPTH, 1, T, 8, DH)
    vv = rows(r["v_out"].reshape(DEPTH, P, CT, T)).reshape(DEPTH, 1, T, 8, DH)
    gl = r["glu_out"].reshape(DEPTH, CT, 2, P, HIST).transpose(0, 2, 4, 1, 3).reshape(DEPTH, 2, 1, HIST, CH)
    ff = r["ffn_out"].reshape(DEPTH, P, FT, 2, 2).transpose(0, 3, 4, 2, 1).reshape(DEPTH, 2, 1, 2, FF)
    res = (y[None, :SEQ], y[None, SEQ:], kk[:, :, :SEQ], vv[:, :, :SEQ], gl[:, 0], ff[:, 0],
           kk[:, :, SEQ:], vv[:, :, SEQ:], gl[:, 1], ff[:, 1], r["sgu_out"].reshape(DEPTH, 1, DEC, CH))
    return tuple(np.ascontiguousarray(v) for v in res)
```
